# Optimizing a Trainium2 kernel written in Bass

```python
import jax, jax.numpy as jnp
from jax import lax
import numpy as np
import math

D_MODEL = 2048
BATCH = 1
SEQ = 256
DEPTH = 2

N_MIXERS = 4
HEAD_DIM = 128
N_HEADS = D_MODEL // HEAD_DIM
N_KV_HEADS = 4
GROUP = N_HEADS // N_KV_HEADS
INNER = N_HEADS * HEAD_DIM
KV_WIDTH = N_KV_HEADS * HEAD_DIM
IDX_HEADS = 16
IDX_DIM = 64
DSA_TOPK = 256
MOBA_BLOCK = 256
MOBA_TOPK = 3
RET_HEADS = 8
RET_QK_DIM = D_MODEL // RET_HEADS
RET_V_DIM = 2 * RET_QK_DIM
RET_INNER = RET_HEADS * RET_V_DIM
RET_CHUNK = 128
Q_BLOCK = 128
ROPE_THETA = 10000.0
EPS = 1e-6
NEG = -1e30

A_WIDTHS = (INNER, KV_WIDTH, KV_WIDTH, INNER, IDX_HEADS * IDX_DIM, IDX_DIM, IDX_HEADS)
B_WIDTHS = (INNER, KV_WIDTH, KV_WIDTH, INNER)
C_WIDTHS = (RET_HEADS * RET_QK_DIM, RET_HEADS * RET_QK_DIM, RET_INNER, RET_INNER)
D_WIDTHS = (INNER, INNER, INNER, INNER, N_HEADS)


def n_layers_of(m):
    return len(range(m, DEPTH, N_MIXERS))

def split_cols(z, widths):
    cuts = [int(c) for c in np.cumsum(widths)[:-1]]
    return jnp.split(z, cuts, axis=-1)

def rms_norm(x, g):
    xf = x.astype(jnp.float32)
    y = xf * lax.rsqrt(jnp.mean(xf * xf, axis=-1, keepdims=True) + EPS)
    return (y * g.astype(jnp.float32)).astype(x.dtype)

def rope(x, pos):
    d = x.shape[-1]
    inv = ROPE_THETA ** (-jnp.arange(0, d, 2, dtype=jnp.float32) / d)
    ang = pos.astype(jnp.float32)[:, None] * inv[None, :]
    cos = jnp.cos(ang)[None, :, None, :]
    sin = jnp.sin(ang)[None, :, None, :]
    x1, x2 = jnp.split(x.astype(jnp.float32), 2, axis=-1)
    return jnp.concatenate([x1 * cos - x2 * sin, x1 * sin + x2 * cos], axis=-1).astype(x.dtype)

def sweep_query_blocks(fn, T):
    starts = jnp.arange(T // Q_BLOCK, dtype=jnp.int32) * Q_BLOCK
    out = lax.map(fn, starts)
    _, B, _, w = out.shape
    return jnp.swapaxes(out, 0, 1).reshape(B, T, w)

def batched_gather(src, idx):
    return jax.vmap(lambda s, i: s[i])(src, idx)

def dsa_mixer(h, w_in, q_g, k_g, w_out):
    B, T, _ = h.shape
    pos = jnp.arange(T, dtype=jnp.int32)
    q, k, v, gate, qi, ki, wi = split_cols(h @ w_in, A_WIDTHS)
    q = rope(rms_norm(q.reshape(B, T, N_HEADS, HEAD_DIM), q_g), pos)
    k = rope(rms_norm(k.reshape(B, T, N_KV_HEADS, HEAD_DIM), k_g), pos)
    v = v.reshape(B, T, N_KV_HEADS, HEAD_DIM)
    qi = rope(qi.reshape(B, T, IDX_HEADS, IDX_DIM), pos).astype(jnp.float32)
    ki = rope(ki.reshape(B, T, 1, IDX_DIM), pos)[:, :, 0].astype(jnp.float32)
    wi = wi.astype(jnp.float32) * IDX_HEADS ** -0.5
    n_keep = min(DSA_TOPK, T // 4)
    scale = HEAD_DIM ** -0.5

    def block(start):
        tq = start + jnp.arange(Q_BLOCK, dtype=jnp.int32)
        qib = lax.dynamic_slice_in_dim(qi, start, Q_BLOCK, axis=1)
        wib = lax.dynamic_slice_in_dim(wi, start, Q_BLOCK, axis=1)
        rel = jax.nn.relu(jnp.einsum('bqhd,bsd->bqhs', qib, ki) * IDX_DIM ** -0.5)
        score = jnp.einsum('bqh,bqhs->bqs', wib, rel)
        causal = pos[None, :] <= tq[:, None]
        score = jnp.where(causal[None], score, NEG)
        _, sel = lax.top_k(score, n_keep)
        valid = sel <= tq[None, :, None]
        k_sel = batched_gather(k, sel)
        v_sel = batched_gather(v, sel)
        qb = lax.dynamic_slice_in_dim(q, start, Q_BLOCK, axis=1).reshape(B, Q_BLOCK, N_KV_HEADS, GROUP, HEAD_DIM)
        logits = jnp.einsum('bqgrd,bqkgd->bqgrk', qb, k_sel).astype(jnp.float32) * scale
        logits = jnp.where(valid[:, :, None, None, :], logits, NEG)
        p = jax.nn.softmax(logits, axis=-1).astype(v.dtype)
        o = jnp.einsum('bqgrk,bqkgd->bqgrd', p, v_sel)
        return o.reshape(B, Q_BLOCK, INNER)

    o = sweep_query_blocks(block, T)
    return (jax.nn.silu(gate) * o) @ w_out

def moba_mixer(h, w_in, q_g, k_g, w_out):
    B, T, _ = h.shape
    pos = jnp.arange(T, dtype=jnp.int32)
    q, k, v, gate = split_cols(h @ w_in, B_WIDTHS)
    q = rope(rms_norm(q.reshape(B, T, N_HEADS, HEAD_DIM), q_g), pos)
    k = rope(rms_norm(k.reshape(B, T, N_KV_HEADS, HEAD_DIM), k_g), pos)
    v = v.reshape(B, T, N_KV_HEADS, HEAD_DIM)
    n_blocks = -(-T // MOBA_BLOCK)
    pad = n_blocks * MOBA_BLOCK - T
    kb = jnp.pad(k, ((0, 0), (0, pad), (0, 0), (0, 0))).reshape(B, n_blocks, MOBA_BLOCK, N_KV_HEADS, HEAD_DIM)
    vb = jnp.pad(v, ((0, 0), (0, pad), (0, 0), (0, 0))).reshape(B, n_blocks, MOBA_BLOCK, N_KV_HEADS, HEAD_DIM)
    k_mean = jnp.mean(kb.astype(jnp.float32), axis=2)
    kbt = kb.transpose(0, 3, 1, 2, 4)
    vbt = vb.transpose(0, 3, 1, 2, 4)
    n_sel = min(MOBA_TOPK, n_blocks - 1)
    gather2 = jax.vmap(jax.vmap(lambda s, i: s[i]))
    scale = HEAD_DIM ** -0.5

    def block(start):
        tq = start + jnp.arange(Q_BLOCK, dtype=jnp.int32)
        own = start // MOBA_BLOCK
        qb = lax.dynamic_slice_in_dim(q, start, Q_BLOCK, axis=1).reshape(B, Q_BLOCK, N_KV_HEADS, GROUP, HEAD_DIM)
        k_own = lax.dynamic_index_in_dim(kb, own, axis=1, keepdims=False)
        v_own = lax.dynamic_index_in_dim(vb, own, axis=1, keepdims=False)
        own_pos = own * MOBA_BLOCK + jnp.arange(MOBA_BLOCK, dtype=jnp.int32)
        l_own = jnp.einsum('bqgrd,bsgd->bqgrs', qb, k_own).astype(jnp.float32) * scale
        l_own = jnp.where((own_pos[None, :] <= tq[:, None])[None, :, None, None, :], l_own, NEG)
        if n_sel == 0:
            p = jax.nn.softmax(l_own, axis=-1).astype(v.dtype)
            o = jnp.einsum('bqgrs,bsgd->bqgrd', p, v_own)
        else:
            gscore = jnp.einsum('bqgrd,bngd->bqgn', qb.astype(jnp.float32), k_mean)
            past = jnp.arange(n_blocks, dtype=jnp.int32) < own
            gscore = jnp.where(past, gscore, NEG)
            _, sel = lax.top_k(gscore, n_sel)
            valid = sel < own
            sel_t = jnp.swapaxes(sel, 1, 2)
            k_sel = gather2(kbt, sel_t)
            v_sel = gather2(vbt, sel_t)
            l_sel = jnp.einsum('bqgrd,bgqnsd->bqgrns', qb, k_sel).astype(jnp.float32) * scale
            l_sel = jnp.where(valid[:, :, :, None, :, None], l_sel, NEG)
            n_k = n_sel * MOBA_BLOCK
            logits = jnp.concatenate([l_sel.reshape(B, Q_BLOCK, N_KV_HEADS, GROUP, n_k), l_own], axis=-1)
            p = jax.nn.softmax(logits, axis=-1).astype(v.dtype)
            p_sel = p[..., :n_k].reshape(B, Q_BLOCK, N_KV_HEADS, GROUP, n_sel, MOBA_BLOCK)
            p_own = p[..., n_k:]
            o = (jnp.einsum('bqgrns,bgqnsd->bqgrd', p_sel, v_sel)
                 + jnp.einsum('bqgrs,bsgd->bqgrd', p_own, v_own))
        return o.reshape(B, Q_BLOCK, INNER)

    o = sweep_query_blocks(block, T)
    return (jax.nn.silu(gate) * o) @ w_out

def retention_mixer(h, w_in, gn_g, w_out):
    B, T, _ = h.shape
    pos = jnp.arange(T, dtype=jnp.int32)
    q, k, v, gate = split_cols(h @ w_in, C_WIDTHS)
    q = rope(q.reshape(B, T, RET_HEADS, RET_QK_DIM), pos).astype(jnp.float32)
    k = rope(k.reshape(B, T, RET_HEADS, RET_QK_DIM), pos).astype(jnp.float32) * RET_QK_DIM ** -0.5
    v = v.reshape(B, T, RET_HEADS, RET_V_DIM).astype(jnp.float32)
    log_gamma = jnp.log(1.0 - 2.0 ** (-5.0 - jnp.arange(RET_HEADS, dtype=jnp.float32)))
    i = jnp.arange(RET_CHUNK, dtype=jnp.float32)
    diff = i[:, None] - i[None, :]
    decay_mask = jnp.where(diff >= 0, jnp.exp(jnp.maximum(diff, 0.0)[None] * log_gamma[:, None, None]), 0.0)
    q_decay = jnp.exp((i[:, None] + 1.0) * log_gamma[None, :])
    k_decay = jnp.exp((RET_CHUNK - 1.0 - i[:, None]) * log_gamma[None, :])
    chunk_decay = jnp.exp(RET_CHUNK * log_gamma)
    n_chunks = T // RET_CHUNK

    def to_chunks(a):
        return jnp.swapaxes(a.reshape(B, n_chunks, RET_CHUNK, *a.shape[2:]), 0, 1)

    def step(state, inp):
        qc, kc, vc = inp
        inner = jnp.einsum('bihd,bjhd->bhij', qc, kc) * decay_mask[None]
        o = (jnp.einsum('bhij,bjhv->bihv', inner, vc)
             + jnp.einsum('bihd,bhdv->bihv', qc * q_decay[None, :, :, None], state))
        state = (state * chunk_decay[None, :, None, None]
                 + jnp.einsum('bjhd,bjhv->bhdv', kc * k_decay[None, :, :, None], vc))
        return state, o

    s0 = jnp.zeros((B, RET_HEADS, RET_QK_DIM, RET_V_DIM), jnp.float32)
    _, o = lax.scan(step, s0, (to_chunks(q), to_chunks(k), to_chunks(v)))
    o = jnp.swapaxes(o, 0, 1).reshape(B, T, RET_HEADS, RET_V_DIM)
    mu = jnp.mean(o, axis=-1, keepdims=True)
    var = jnp.mean(jnp.square(o - mu), axis=-1, keepdims=True)
    o = ((o - mu) * lax.rsqrt(var + EPS)).reshape(B, T, RET_INNER) * gn_g.astype(jnp.float32)
    return (jax.nn.silu(gate) * o.astype(h.dtype)) @ w_out

def fox_mixer(h, w_in, f_bias, q_g, k_g, w_out):
    B, T, _ = h.shape
    pos = jnp.arange(T, dtype=jnp.int32)
    q, k, v, gate, f_logit = split_cols(h @ w_in, D_WIDTHS)
    q = rms_norm(q.reshape(B, T, N_HEADS, HEAD_DIM), q_g)
    k = rms_norm(k.reshape(B, T, N_HEADS, HEAD_DIM), k_g)
    v = v.reshape(B, T, N_HEADS, HEAD_DIM)
    log_f = jax.nn.log_sigmoid((f_logit + f_bias).astype(jnp.float32))
    cum_t = jnp.swapaxes(lax.cumsum(log_f, axis=1), 1, 2)
    scale = HEAD_DIM ** -0.5

    def block(start):
        tq = start + jnp.arange(Q_BLOCK, dtype=jnp.int32)
        qb = lax.dynamic_slice_in_dim(q, start, Q_BLOCK, axis=1)
        cq = lax.dynamic_slice_in_dim(cum_t, start, Q_BLOCK, axis=2)
        logits = (jnp.einsum('bqhd,bshd->bhqs', qb, k).astype(jnp.float32) * scale
                  + cq[..., None] - cum_t[:, :, None, :])
        logits = jnp.where((pos[None, :] <= tq[:, None])[None, None], logits, NEG)
        p = jax.nn.softmax(logits, axis=-1).astype(v.dtype)
        o = jnp.einsum('bhqs,bshd->bqhd', p, v)
        return o.reshape(B, Q_BLOCK, INNER)

    o = sweep_query_blocks(block, T)
    return (jax.nn.silu(gate) * o) @ w_out

def first_inputs(seed: int = 0) -> dict:
    key = jax.random.key(seed)
    ks = jax.random.split(key, 21)
    nA, nB, nC, nD = (n_layers_of(m) for m in range(N_MIXERS))

    def dense(k, shape, fan_in):
        return jax.random.normal(k, shape, jnp.float32) * fan_in ** -0.5

    def gain(k, shape):
        return 1.0 + 0.02 * jax.random.normal(k, shape, jnp.float32)

    return {
        'x': jax.random.normal(ks[0], (BATCH, SEQ, D_MODEL), jnp.float32),
        'a_norm': gain(ks[1], (nA, D_MODEL)),
        'a_w_in': dense(ks[2], (nA, D_MODEL, sum(A_WIDTHS)), D_MODEL),
        'a_q_norm': gain(ks[3], (nA, HEAD_DIM)),
        'a_k_norm': gain(ks[4], (nA, HEAD_DIM)),
        'a_w_out': dense(ks[5], (nA, INNER, D_MODEL), INNER),
        'b_norm': gain(ks[6], (nB, D_MODEL)),
        'b_w_in': dense(ks[7], (nB, D_MODEL, sum(B_WIDTHS)), D_MODEL),
        'b_q_norm': gain(ks[8], (nB, HEAD_DIM)),
        'b_k_norm': gain(ks[9], (nB, HEAD_DIM)),
        'b_w_out': dense(ks[10], (nB, INNER, D_MODEL), INNER),
        'c_norm': gain(ks[11], (nC, D_MODEL)),
        'c_w_in': dense(ks[12], (nC, D_MODEL, sum(C_WIDTHS)), D_MODEL),
        'c_gn': gain(ks[13], (nC, RET_INNER)),
        'c_w_out': dense(ks[14], (nC, RET_INNER, D_MODEL), RET_INNER),
        'd_norm': gain(ks[15], (nD, D_MODEL)),
        'd_w_in': dense(ks[16], (nD, D_MODEL, sum(D_WIDTHS)), D_MODEL),
        'd_f_bias': jax.random.uniform(ks[17], (nD, N_HEADS), jnp.float32, minval=1.0, maxval=4.0),
        'd_q_norm': gain(ks[18], (nD, HEAD_DIM)),
        'd_k_norm': gain(ks[19], (nD, HEAD_DIM)),
        'd_w_out': dense(ks[20], (nD, INNER, D_MODEL), INNER),
    }

def first_block(x, a_norm, a_w_in, a_q_norm, a_k_norm, a_w_out,
              b_norm, b_w_in, b_q_norm, b_k_norm, b_w_out,
              c_norm, c_w_in, c_gn, c_w_out,
              d_norm, d_w_in, d_f_bias, d_q_norm, d_k_norm, d_w_out):
    h = x
    for i in range(DEPTH):
        m = i % N_MIXERS
        j = i // N_MIXERS
        if m == 0:
            h = h + dsa_mixer(rms_norm(h, a_norm[j]), a_w_in[j], a_q_norm[j], a_k_norm[j], a_w_out[j])
        elif m == 1:
            h = h + moba_mixer(rms_norm(h, b_norm[j]), b_w_in[j], b_q_norm[j], b_k_norm[j], b_w_out[j])
        elif m == 2:
            h = h + retention_mixer(rms_norm(h, c_norm[j]), c_w_in[j], c_gn[j], c_w_out[j])
        else:
            h = h + fox_mixer(rms_norm(h, d_norm[j]), d_w_in[j], d_f_bias[j], d_q_norm[j], d_k_norm[j], d_w_out[j])
    return h


DEPTH_2 = 1

N_MEM = 256
MIX_W = D_MODEL // 2
GLA_HEADS = 4
GLA_DV = MIX_W // GLA_HEADS
GLA_DK = GLA_DV // 2
GLA_RANK = 16
GLA_TAU = 16.0
GLA_CHUNK = 64
SB_HEADS = 8
SB_DH = MIX_W // SB_HEADS
SB_BLOCK = 128
MEM_HEADS = 4
MEM_DH = MIX_W // MEM_HEADS
N_BRANCH = 3
D_FF = int(math.ceil(8 * D_MODEL / 3 / 256) * 256)

SPLIT_SIZES = [
    GLA_HEADS * GLA_DK,
    GLA_HEADS * GLA_DK,
    GLA_HEADS * GLA_DV,
    GLA_HEADS * GLA_DV,
    GLA_RANK,
    SB_HEADS * SB_DH,
    SB_HEADS * SB_DH,
    SB_HEADS * SB_DH,
    MEM_HEADS * MEM_DH,
    N_BRANCH * D_MODEL,
]
IN_W = int(sum(SPLIT_SIZES))
SPLIT_POINTS = [int(p) for p in np.cumsum(SPLIT_SIZES)[:-1]]


def rmsnorm(x, g):
    xf = x.astype(jnp.float32)
    y = xf * lax.rsqrt(jnp.mean(xf * xf, axis=-1, keepdims=True) + EPS)
    return (y * g.astype(jnp.float32)).astype(x.dtype)

def gla_mixer(q, k, v, log_a):
    B, T, H, dk = q.shape
    dv = v.shape[-1]
    N = T // GLA_CHUNK

    def chunk(a):
        return a.astype(jnp.float32).reshape(B, N, GLA_CHUNK, H, a.shape[-1]).transpose(0, 3, 1, 2, 4)

    qc = chunk(q) * (dk ** -0.5)
    kc, vc, gc = chunk(k), chunk(v), chunk(log_a)
    b = jnp.cumsum(gc, axis=3)
    b_last = b[:, :, :, -1:, :]
    q_e = qc * jnp.exp(b)
    k_e = kc * jnp.exp(-b)
    k_d = kc * jnp.exp(b_last - b)
    decay = jnp.exp(b_last[:, :, :, 0, :])

    causal = jnp.tril(jnp.ones((GLA_CHUNK, GLA_CHUNK), dtype=bool))
    s = jnp.where(causal, jnp.einsum('bhncd,bhnsd->bhncs', q_e, k_e), 0.0)
    o_intra = jnp.einsum('bhncs,bhnsv->bhncv', s, vc)

    def step(S, inp):
        qe, kd, vv, dec = inp
        o = jnp.einsum('bhcd,bhdv->bhcv', qe, S)
        S = S * dec[..., :, None] + jnp.einsum('bhcd,bhcv->bhdv', kd, vv)
        return S, o

    xs = (jnp.moveaxis(q_e, 2, 0), jnp.moveaxis(k_d, 2, 0), jnp.moveaxis(vc, 2, 0), jnp.moveaxis(decay, 2, 0))
    S0 = jnp.zeros((B, H, dk, dv), jnp.float32)
    _, o_inter = lax.scan(step, S0, xs)
    o = o_intra + jnp.moveaxis(o_inter, 0, 2)
    return o.transpose(0, 2, 3, 1, 4).reshape(B, T, H, dv)

def stick_breaking_mixer(q, k, v):
    B, T, H, d = q.shape
    NB = T // SB_BLOCK
    scale = d ** -0.5
    qt = q.transpose(0, 2, 1, 3)
    kt = k.transpose(0, 2, 1, 3)
    vt = v.transpose(0, 2, 1, 3)
    idx = jnp.arange(SB_BLOCK)
    later = (idx[:, None] > idx[None, :]).astype(jnp.float32)
    outs = []
    for i in range(NB):
        L = (i + 1) * SB_BLOCK
        qi = qt[:, :, i * SB_BLOCK:L]
        kb = kt[:, :, :L]
        vb = vt[:, :, :L]
        z = jnp.einsum('bhqd,bhkd->bhqk', qi, kb).astype(jnp.float32) * scale
        mask = jnp.arange(L)[None, :] < (i * SB_BLOCK + idx)[:, None]
        l = jnp.where(mask, jax.nn.log_sigmoid(-z), 0.0).reshape(B, H, SB_BLOCK, i + 1, SB_BLOCK)
        within = jnp.einsum('bhqnj,js->bhqns', l, later)
        tot = jnp.sum(l, axis=-1)
        after = lax.cumsum(tot, axis=3, reverse=True) - tot
        rest = (within + after[..., None]).reshape(B, H, SB_BLOCK, L)
        A = jnp.where(mask, jnp.exp(jax.nn.log_sigmoid(z) + rest), 0.0)
        outs.append(jnp.einsum('bhqk,bhkd->bhqd', A.astype(vb.dtype), vb))
    out = jnp.concatenate(outs, axis=2)
    return out.transpose(0, 2, 1, 3).reshape(B, T, H * d)

def memory_mixer(q, mem_k, mem_v):
    B, T, H, d = q.shape
    s = jnp.einsum('bthd,bmhd->bhtm', q, mem_k).astype(jnp.float32) * (d ** -0.5)
    p = jax.nn.softmax(s, axis=-1)
    o = jnp.einsum('bhtm,bmhd->bthd', p.astype(mem_v.dtype), mem_v)
    return o.reshape(B, T, H * d)

def second_inputs(seed: int = 0) -> dict:
    key = jax.random.key(seed)
    ks = jax.random.split(key, 24)
    L, D = DEPTH_2, D_MODEL

    def w(k, shape, fan_in):
        return jax.random.normal(k, shape, jnp.float32) * (fan_in ** -0.5)

    def gain(k, shape):
        return 1.0 + 0.02 * jax.random.normal(k, shape, jnp.float32)

    return {
        "x": jax.random.normal(ks[0], (BATCH, SEQ, D), jnp.float32),
        "mem": jax.random.normal(ks[1], (BATCH, N_MEM, D), jnp.float32),
        "attn_norm": gain(ks[2], (L, D)),
        "w_in": w(ks[3], (L, D, IN_W), D),
        "gla_w_a2": w(ks[4], (L, GLA_RANK, GLA_HEADS * GLA_DK), GLA_RANK),
        "gla_b_a": 0.1 * jax.random.normal(ks[5], (L, GLA_HEADS * GLA_DK), jnp.float32),
        "gla_out_norm": gain(ks[6], (L, GLA_DV)),
        "w_br_gla": w(ks[7], (L, GLA_HEADS * GLA_DV, D), GLA_HEADS * GLA_DV),
        "sb_q_norm": gain(ks[8], (L, SB_DH)),
        "sb_k_norm": gain(ks[9], (L, SB_DH)),
        "w_br_sb": w(ks[10], (L, SB_HEADS * SB_DH, D), SB_HEADS * SB_DH),
        "mem_norm": gain(ks[11], (L, D)),
        "w_mem_kv": w(ks[12], (L, D, 2 * MEM_HEADS * MEM_DH), D),
        "mem_q_norm": gain(ks[13], (L, MEM_DH)),
        "mem_k_norm": gain(ks[14], (L, MEM_DH)),
        "w_br_mem": w(ks[15], (L, MEM_HEADS * MEM_DH, D), MEM_HEADS * MEM_DH),
        "w_o": w(ks[16], (L, D, D), D),
        "ffn_norm": gain(ks[17], (L, D)),
        "w_gate_up": w(ks[18], (L, D, 2 * D_FF), D),
        "w_down": w(ks[19], (L, D_FF, D), D_FF),
    }

def second_block(x, mem, attn_norm, w_in, gla_w_a2, gla_b_a, gla_out_norm, w_br_gla,
              sb_q_norm, sb_k_norm, w_br_sb, mem_norm, w_mem_kv, mem_q_norm, mem_k_norm,
              w_br_mem, w_o, ffn_norm, w_gate_up, w_down):
    B, T, D = x.shape
    M = mem.shape[1]
    for l in range(DEPTH_2):
        h = rmsnorm(x, attn_norm[l])
        proj = h @ w_in[l]
        (gq, gk, gv, gr, ga1, sq, sk, sv, mq, gates) = jnp.split(proj, SPLIT_POINTS, axis=-1)

        log_a = jax.nn.log_sigmoid((ga1 @ gla_w_a2[l] + gla_b_a[l]).astype(jnp.float32)) / GLA_TAU
        o_gla = gla_mixer(gq.reshape(B, T, GLA_HEADS, GLA_DK), gk.reshape(B, T, GLA_HEADS, GLA_DK),
                          gv.reshape(B, T, GLA_HEADS, GLA_DV), log_a.reshape(B, T, GLA_HEADS, GLA_DK))
        o_gla = rmsnorm(o_gla, gla_out_norm[l]).reshape(B, T, GLA_HEADS * GLA_DV).astype(x.dtype)
        y_gla = (o_gla * jax.nn.silu(gr)) @ w_br_gla[l]

        q_sb = rmsnorm(sq.reshape(B, T, SB_HEADS, SB_DH), sb_q_norm[l])
        k_sb = rmsnorm(sk.reshape(B, T, SB_HEADS, SB_DH), sb_k_norm[l])
        y_sb = stick_breaking_mixer(q_sb, k_sb, sv.reshape(B, T, SB_HEADS, SB_DH)) @ w_br_sb[l]

        mem_kv = rmsnorm(mem, mem_norm[l]) @ w_mem_kv[l]
        m_k, m_v = jnp.split(mem_kv, 2, axis=-1)
        m_k = rmsnorm(m_k.reshape(B, M, MEM_HEADS, MEM_DH), mem_k_norm[l])
        m_v = m_v.reshape(B, M, MEM_HEADS, MEM_DH)
        q_m = rmsnorm(mq.reshape(B, T, MEM_HEADS, MEM_DH), mem_q_norm[l])
        y_mem = memory_mixer(q_m, m_k, m_v) @ w_br_mem[l]

        g = jax.nn.sigmoid(gates.reshape(B, T, N_BRANCH, D))
        merged = g[:, :, 0] * y_gla + g[:, :, 1] * y_sb + g[:, :, 2] * y_mem
        x = x + merged @ w_o[l]

        h2 = rmsnorm(x, ffn_norm[l])
        gate, up = jnp.split(h2 @ w_gate_up[l], 2, axis=-1)
        x = x + (jax.nn.silu(gate) * up) @ w_down[l]
    return x


def setup_inputs(seed=0):
    out = dict(first_inputs(seed))
    for name, value in second_inputs(seed + 1).items():
        if name != "x":
            out[name + "_2"] = value
    return out


def reference(
    x, a_norm, a_w_in, a_q_norm, a_k_norm, a_w_out, b_norm, b_w_in, b_q_norm, b_k_norm, b_w_out,
    c_norm, c_w_in, c_gn, c_w_out, d_norm, d_w_in, d_f_bias, d_q_norm, d_k_norm, d_w_out, mem_2,
    attn_norm_2, w_in_2, gla_w_a2_2, gla_b_a_2, gla_out_norm_2, w_br_gla_2, sb_q_norm_2,
    sb_k_norm_2, w_br_sb_2, mem_norm_2, w_mem_kv_2, mem_q_norm_2, mem_k_norm_2, w_br_mem_2,
    w_o_2, ffn_norm_2, w_gate_up_2, w_down_2,
):
    x = first_block(
        x, a_norm, a_w_in, a_q_norm, a_k_norm, a_w_out, b_norm, b_w_in, b_q_norm, b_k_norm,
        b_w_out, c_norm, c_w_in, c_gn, c_w_out, d_norm, d_w_in, d_f_bias, d_q_norm, d_k_norm,
        d_w_out,
    )
    return second_block(
        x, mem_2, attn_norm_2, w_in_2, gla_w_a2_2, gla_b_a_2, gla_out_norm_2, w_br_gla_2,
        sb_q_norm_2, sb_k_norm_2, w_br_sb_2, mem_norm_2, w_mem_kv_2, mem_q_norm_2, mem_k_norm_2,
        w_br_mem_2, w_o_2, ffn_norm_2, w_gate_up_2, w_down_2,
    )


_drawn_inputs = setup_inputs


def setup_inputs(seed=0):
    import zlib

    import numpy as np

    out = dict(_drawn_inputs(seed))
    spreads = {}
    factors = {'a_q_norm': 8.0,
     'a_k_norm': 8.0,
     'b_norm': 8.0,
     'b_q_norm': 8.0,
     'b_k_norm': 8.0,
     'attn_norm_2': 9.866,
     'gla_b_a_2': 4.2,
     'gla_out_norm_2': 64.0,
     'sb_q_norm_2': 200.0,
     'sb_k_norm_2': 200.0,
     'mem_norm_2': 108.352,
     'mem_q_norm_2': 26.526,
     'mem_k_norm_2': 94.482,
     'ffn_norm_2': 32.421}
    for name, (base, spread) in spreads.items():
        noise = np.random.default_rng([zlib.crc32(name.encode()), seed]).standard_normal(out[name].shape)
        drawn = base * np.exp(spread * noise) if base else spread * noise
        out[name] = __import__('jax').numpy.asarray(drawn.astype(out[name].dtype))
    for name, factor in factors.items():
        out[name] = (out[name] * factor).astype(out[name].dtype)
    return out
```

```python
from contextlib import ExitStack

import numpy as np
import concourse.bass as bass
from concourse import mybir

F32 = mybir.dt.float32
F32R = mybir.dt.float32r
I32 = mybir.dt.int32
ALU = mybir.AluOpType
ACT = mybir.ActivationFunctionType
AX = mybir.AxisListType

P = 128
T = 256
TT = T // P
D = 2048
KT = D // P
NB = 512
KC = 4
RAW = 2
SPL = 4
LEAD = 2
HD = 128
GROUPS = 4
HPG = 4
EPS = 1e-6
NEG = -1e30
TAKEN = -3e38
SCALE = float(HD) ** -0.5
N_KEEP = T // 4
IDX_HEADS, IDX_DIM = 16, 64
W0 = P + T
RSQRT_SEED = 1597463007.0

A_COLS = dict(q=0, k=2048, v=2560, gate=3072, qi=5120, ki=6144)
F_FF = 5632
FF_PARTS = ((0, 4), (4, 4), (8, 3))
GLA_HEADS, GLA_DK, GLA_DV, GLA_CHUNK, GLA_TAU = 4, 128, 256, 64, 16.0
SB_HEADS, MEM_HEADS, MEM_DH = 8, 4, 256
MIX_KC = 1024 // P // KC
IN_COLS = dict(gq=0, gk=512, gv=1024, gr=2048, ga=3072, sq=3088, sk=4112, sv=5136, mq=6160, gates=7184)
BIG = 3e38
B_COLS = dict(q=0, k=2048, v=2560, gate=3072)


class Count:

    def __init__(self, k=0):
        self.k, self.reg = k, None

    def __call__(self, d=0):
        v = self.k + d
        return v if self.reg is None else self.reg + v

    def step(self, n=1):
        self.k += n


def loop(eng, start, end, steps):
    with eng.Fori(start, end) as j:
        first = {c: c.k for c in steps}
        for c, per in steps.items():
            assert c.reg is None
            c.reg = (j - start) * per if start else j * per
        yield j
        for c, per in steps.items():
            assert c.k - first[c] == per, (c.k, first[c], per)
            c.reg, c.k = None, first[c] + per * (end - start)


def constants():
    def table(d):
        inv = (10000.0 ** (-np.arange(0, d, 2, dtype=np.float32) / np.float32(d))).astype(np.float32)
        ang = np.arange(T, dtype=np.float32)[:, None] * inv[None, :]
        c, s = np.cos(ang), np.sin(ang)
        both = np.stack([np.concatenate([c, c], 1), np.concatenate([-s, s], 1)])
        return both.reshape(2, TT, P, d).transpose(2, 0, 1, 3).astype(np.float32)

    i = np.arange(P)
    chunk = i // 64
    same = chunk[:, None] == chunk[None, :]
    causal = np.where(i[None, :] <= i[:, None], 0.0, NEG)
    mask = np.concatenate([causal, np.zeros((P, P)), causal], 1)
    squares = np.stack([
        np.eye(P),
        same & (i[:, None] <= i[None, :]),
        same & (i[:, None] > i[None, :]),
        i[:, None] > i[None, :],
        np.ones((P, P)),
        i[:, None] < i[None, :],
        np.where(i[:, None] <= i[None, :], BIG, 0.0),
        np.where(i[:, None] <= i[None, :], -BIG, 0.0),
    ]).astype(np.float32)
    ends = np.stack([chunk == 0, chunk == 1], 1).astype(np.float32)
    return {
        "c_rope128": table(HD), "c_rope64": table(IDX_DIM), "c_mask": mask.astype(np.float32),
        "c_squares": np.ascontiguousarray(squares.transpose(1, 0, 2)), "c_ends": ends,
    }


def program(nc, io, out):
    ctx = ExitStack()
    with ctx:
        base = (nc.sbuf_base + 63) // 64 * 64
        top = [base]

        def at(name, shape, offset, dt=F32):
            return nc.alloc_sbuf_tensor_at(name, shape, dt, offset=offset)

        def sb(name, shape, dt=F32):
            n = 4
            for s in shape[1:]:
                n *= s
            t = at(name, shape, top[0], dt)
            top[0] += (n + 31) // 32 * 32
            assert top[0] <= nc.sbuf_usable_end, (name, top[0])
            return t

        def sem(name):
            return ctx.enter_context(nc.semaphore(name))

        N_GAINS = 5 * KT + 6
        MEM_Q, MEM_K, SB_Q, SB_K = 5 * KT, 5 * KT + 2, 5 * KT + 4, 5 * KT + 5
        raw = sb("raw", [P, RAW, KC, NB])
        w_hi = sb("w_hi", [P, SPL, KC, NB], F32R)
        w_lo = sb("w_lo", [P, SPL, KC, NB], F32R)
        a_hi = [sb("a0_hi", [P, KT, T], F32R)]
        a_lo = [sb("a0_lo", [P, KT, T], F32R)]
        a1_at = top[0]
        a_hi.append(sb("a1_hi", [P, KT, T], F32R))
        a_lo.append(sb("a1_lo", [P, KT, T], F32R))
        base_x = top[0]
        x = sb("x", [P, TT, D])
        ident_t = sb("ident", [P, P])
        ident = ident_t[:]
        ends = sb("ends", [P, 2])
        gains = sb("gains", [P, N_GAINS])
        ss = sb("ss", [P, TT])
        ss_part = sb("ss_part", [P, 2, TT])
        rstd = sb("rstd", [P, TT])
        newton = sb("newton", [P, 4, 16])
        arena2 = top[0]
        rope = sb("rope", [P, 2, TT, HD])
        cmask = sb("cmask", [P, W0])
        qk_gain = sb("qk_gain", [P, 2, HD])
        rope_q = sb("rope_q", [P, 2, TT, HD])
        rope_k = sb("rope_k", [P, 2, TT, HD])
        arena = top[0]

        def area(name, shape, offset, dt=F32):
            n = 4
            for s in shape[1:]:
                n *= s
            assert arena + offset + n <= nc.sbuf_usable_end, (name, arena + offset + n, nc.sbuf_usable_end)
            return at(name, shape, arena + offset, dt)

        K = 1024
        kT = area("kT", [P, GROUPS, T], 0)
        v_nat = area("v_nat", [P, TT, GROUPS * HD], 4 * K)
        proj = area("proj", [P, TT, NB], 8 * K)
        rot = area("rot", [P, TT, NB], 12 * K)
        qT = area("qT", [P, HPG, T], 16 * K)
        rope_t = area("rope_t", [P, TT, NB], 16 * K)
        silu_g = area("silu_g", [P, TT, NB], 20 * K)
        o_gated = area("o_gated", [P, TT, NB], 24 * K)
        probs = area("probs", [P, 2, W0], 28 * K)
        probsT = area("probsT", [P, 2, W0], 31 * K)
        sel_mask = area("sel_mask", [P, W0], 34 * K)
        row = area("row", [P, 4, 2 * HPG], 35 * K + 512)
        qiT = at("qiT", [P, IDX_HEADS // 2, T], a1_at)
        kiT = at("kiT", [P, T], a1_at + 8 * K)
        ki2 = at("ki2", [P, TT, P], a1_at + 9 * K)
        rope64 = at("rope64", [P, 2, TT, IDX_DIM], a1_at + 10 * K)
        wi = at("wi", [P, TT, IDX_HEADS], a1_at + 11 * K)
        relus = at("relus", [P, 2, W0], a1_at + 12 * K)
        score = at("score", [P, W0], a1_at + 15 * K)
        top8 = at("top8", [P, 8], a1_at + 17 * K)
        def area2(name, shape, offset, dt=F32):
            n = 4
            for s in shape[1:]:
                n *= s
            assert arena2 + offset + n <= nc.sbuf_usable_end, (name, arena2 + offset + n, nc.sbuf_usable_end)
            return at(name, shape, arena2 + offset, dt)

        a1_hi_end, a1_lo_end = a1_at + 8 * K, a1_at + 24 * K
        sq = area2("squares", [P, 7, P], 42 * K + 512)
        cum64, after64, after, ones, strict, at_most, at_least = (sq[:, n, :] for n in range(7))
        mem_nat = area2("mem_nat", [P, TT, D], 24 * K)
        mkT = area2("mkT", [P, KT // 2, T], 0)
        mv = area2("mv", [P, TT, 1024], 8 * K)
        mqT = area2("mqT", [P, KT // 2, T], 16 * K)
        pre = area2("pre", [P, TT, NB], 24 * K)
        pre_t = area2("pre_t", [P, TT, NB], 28 * K)
        m_probs = area2("m_probs", [P, 2, TT, T], 32 * K)
        m_probsT = area2("m_probsT", [P, 2, TT, T], 36 * K)
        stat = area2("stat", [P, 4, 8], 40 * K)
        mem_ss = area2("mem_ss", [P, TT], 40 * K + 256)
        mem_rstd = area2("mem_rstd", [P, TT], 40 * K + 288)
        gq = area2("gq", [P, TT, NB], 0)
        gk = area2("gk", [P, TT, NB], 4 * K)
        gv = at("gv", [P, TT, 1024], a1_hi_end)
        gr = at("gr", [P, TT, 1024], a1_lo_end)
        log_a = area2("log_a", [P, NB], 8 * K)
        e_in = area2("e_in", [P, NB], 10 * K)
        e_neg = area2("e_neg", [P, NB], 12 * K)
        e_rest = area2("e_rest", [P, NB], 14 * K)
        kd = area2("kd", [P, NB], 16 * K)
        qeT = area2("qeT", [P, NB], 18 * K)
        keT = area2("keT", [P, NB], 20 * K)
        sT = area2("sT", [P, NB], 22 * K)
        state = area2("state", [P, GLA_HEADS, GLA_DV], 24 * K)
        g_out = area2("g_out", [P, GLA_HEADS, GLA_DV], 28 * K)
        g_sq = area2("g_sq", [P, GLA_HEADS, GLA_DV], 32 * K)
        w_a2 = area2("w_a2", [16, NB], 36 * K)
        b_a = area2("b_a", [P, NB], 38 * K)
        g_gain = area2("g_gain", [P, GLA_DV], 40 * K)
        gaT = area2("gaT", [16, T], 41 * K)
        ga = area2("ga", [P, TT, 16], 42 * K)
        decay = area2("decay", [P, TT, GLA_HEADS, 2], 42 * K + 128)
        sq_nat = at("sq_nat", [P, TT, 1024], a1_hi_end)
        sk_nat = at("sk_nat", [P, TT, 1024], a1_lo_end)
        sv_nat = area2("sv_nat", [P, TT, 1024], 0)
        sb_tmp = area2("sb_tmp", [P, TT, NB], 8 * K)
        qkT = area2("qkT", [P, 2, 2, T], 12 * K)
        soft_p = area2("soft_p", [P, 2, W0], 16 * K)
        neg_l = area2("neg_l", [P, 2, W0], 19 * K)
        stick = area2("stick", [P, 2, W0], 22 * K)
        sb_gain = area2("sb_gain", [P, 2], 25 * K)
        b_gate = area2("b_gate", [P, 2, TT, NB], 28 * K)
        pre_q = at("pre_q", [P, TT, NB], base_x)
        stat2 = area2("stat2", [P, 1], 42 * K + 256)
        decay2 = area2("decay2", [P, 1], 42 * K + 288)
        stat3 = area2("stat3", [P, 1], 42 * K + 320)
        stat4 = area2("stat4", [P, 1], 42 * K + 352)
        b_tmp = area2("b_tmp", [P, TT, NB], 36 * K)
        f_gate = area2("f_gate", [P, TT, NB], 0)
        f_mid = area2("f_mid", [P, TT, NB], 4 * K)
        x_mid = nc.dram_tensor("x_mid", (P, TT, D), F32, kind="Internal").ap()
        x_new = area("x_new", [P, 2, TT, NB], 8 * K)
        row_sq2 = at("row_sq2", [P, TT, D], a1_at)
        junk = area("junk", [P, 2, TT, NB], 16 * K)
        row_sq = area("row_sq", [P, TT, D], 0)
        gain_rows = area("gain_rows", [N_GAINS, P], 20 * K)

        N_CONST = 16

        def chunk_loads(c, d):
            n = 16 * ((c.k + d) // RAW + 1)
            return n if c.reg is None else c.reg * (16 // RAW) + n

        def bank(name):
            return ctx.enter_context(nc.psum_tensor(name, [P, NB], F32))

        G = [[bank(f"gemm{b}_{t}") for t in range(TT)] for b in range(2)]
        M = [bank("turn0"), bank("turn1")]
        L = bank("logits")
        O = bank("mixed")

        raw_in = [sem(f"raw_in{s}") for s in range(RAW)]
        hi_done, lo_done, chunk_done = sem("hi_done"), sem("lo_done"), sem("chunk_done")
        block_read = sem("block_read")
        m_full, m_hi, m_free = sem("m_full"), sem("m_hi"), sem("m_free")
        l_full, l_free = sem("l_full"), sem("l_free")
        o_full, o_free = sem("o_full"), sem("o_free")
        const_in, x_in, table_in = sem("const_in"), sem("x_in"), sem("table_in")
        a_seq = sem("a_seq")
        v_seq = sem("v_seq")
        rot_ready = sem("rot_ready")
        max_ready, probs_ready = sem("max_ready"), sem("probs_ready")
        gate_ready, silu_ready = sem("gate_ready"), sem("silu_ready")
        relu_ready = sem("relu_ready")
        xn_kept = sem("xn_kept")
        squares_ready = sem("squares_ready")
        gains_free = sem("gains_free")
        out_done = sem("out_done")
        for_act, from_act = sem("for_act"), sem("from_act")
        for_pe = sem("for_pe")
        sig_ready = sem("sig_ready")
        mem_in, small_in, x_kept, x_back = sem("mem_in"), sem("small_in"), sem("x_kept"), sem("x_back")
        x_final = sem("x_final")
        phase_done = sem("phase_done")

        def chunks_of(w):
            return w.rearrange("(c k p) n -> p c k n", p=P, k=KC)

        wA, wAo, wB, wBo = (chunks_of(io[n][0]) for n in ("a_w_in", "a_w_out", "b_w_in", "b_w_out"))
        w_in, w_kv, w_o, w_gu, w_dn = (chunks_of(io[n][0]) for n in ("w_in", "w_kv", "w_o", "w_gate_up", "w_down"))
        w_branch = [chunks_of(io[n][0]) for n in ("w_gla", "w_sb", "w_mem")]
        w_gates = [w_in[:, :, :, IN_COLS["gates"] + n * D:IN_COLS["gates"] + (n + 1) * D] for n in range(3)]
        N_CHUNKS = 124 + 8 + 16 + 28 + 24 + 3 * 24 + 16 + 11 * 8 + 44

        block = ctx.enter_context(nc.Block())

        @block.sync
        def _(sp):
            c = Count()

            def load(view, kc, col, width=NB):
                s = c.k % RAW
                if c.k >= RAW:
                    sp.wait_ge(lo_done, c(1 - RAW))
                sp.dma_start(raw[:, s, :, 0:width], view[:, kc, :, bass.ds(col, width)]).then_inc(raw_in[s], 16)
                c.step()

            def load_block(view, col, width=NB):
                for kc in range(KT // KC):
                    load(view, kc, col, width)

            for t in range(TT):
                sp.dma_start(x[:, t, :], io["x"][0, t * P:(t + 1) * P, :]).then_inc(x_in, 16)
            for name in ("k", "v"):
                load_block(wA, A_COLS[name])
            for b in range(2):
                load_block(wA, A_COLS["qi"] + b * NB)
            load_block(wA, A_COLS["ki"], 80)
            for cols, w, w_out in ((A_COLS, wA, wAo), (B_COLS, wB, wBo)):
                if w is wB:
                    load_block(w, cols["k"])
                    load_block(w, cols["v"])
                for j in loop(sp, 0, GROUPS, {c: 8}):
                    load_block(w, cols["q"] + j * NB)
                    load_block(w, cols["gate"] + j * NB)
                for j in loop(sp, 0, 2, {c: 8}):
                    for u in range(2):
                        load_block(w_out, j * (2 * NB) + u * NB)
            for b in range(2):
                load_block(w_in, IN_COLS["mq"] + b * NB)
            for b in range(4):
                load_block(w_kv, b * NB)

            def load_branch(n):
                for j in loop(sp, 0, 2, {c: 12}):
                    for u in range(2):
                        col = j * (2 * NB) + u * NB
                        load_block(w_gates[n], col)
                        for kc in range(MIX_KC):
                            load(w_branch[n], kc, j * NB * 2 + u * NB)

            load_branch(2)
            for b in range(6):
                load_block(w_in, IN_COLS["gq"] + b * NB)
            load_block(w_in, IN_COLS["ga"], 16)
            load_branch(0)
            for b in range(6):
                load_block(w_in, IN_COLS["sq"] + b * NB)
            load_branch(1)
            for j in loop(sp, 0, 2, {c: 8}):
                for u in range(2):
                    load_block(w_o, j * (2 * NB) + u * NB)
            for b0, n in FF_PARTS:
                if n == 4:
                    for j in loop(sp, 0, n, {c: 8}):
                        load_block(w_gu, j * NB + b0 * NB)
                        load_block(w_gu, j * NB + (F_FF + b0 * NB))
                    for j in loop(sp, 0, 2, {c: 8}):
                        for u in range(2):
                            for kc in range(n):
                                load(w_dn, b0 + kc, j * (2 * NB) + u * NB)
                else:
                    for b in range(b0, b0 + n):
                        load_block(w_gu, b * NB)
                        load_block(w_gu, F_FF + b * NB)
                    for b in range(D // NB):
                        for kc in range(n):
                            load(w_dn, b0 + kc, b * NB)
            assert c.k == N_CHUNKS, (c.k, N_CHUNKS)
            out_t = out[0].rearrange("(t p) d -> p t d", p=P)
            for b in range(D // NB):
                sp.wait_ge(x_final, b + 1)
                sp.dma_start(out_t[:, :, b * NB:(b + 1) * NB], x[:, :, b * NB:(b + 1) * NB]).then_inc(out_done, 16)
            sp.wait_ge(out_done, 16 * (D // NB))

        @block.gpsimd
        def _(pool):
            n = 0
            for dst, src in (
                (ident_t[:], io["c_squares"][:, 0, :]), (ends[:], io["c_ends"]), (rope[:], io["c_rope128"]), (cmask[:], io["c_mask"]),
                (rope64[:], io["c_rope64"]),
                (gain_rows[0:16, :], io["a_norm"][0].rearrange("(k p) -> k p", p=P)),
                (gain_rows[16:32, :], io["b_norm"][0].rearrange("(k p) -> k p", p=P)),
                (gain_rows[32:48, :], io["attn_norm_2"][0].rearrange("(k p) -> k p", p=P)),
                (gain_rows[48:64, :], io["mem_norm_2"][0].rearrange("(k p) -> k p", p=P)),
                (gain_rows[64:80, :], io["ffn_norm_2"][0].rearrange("(k p) -> k p", p=P)),
                (gain_rows[MEM_Q:MEM_Q + 2, :], io["mem_q_norm"][0].rearrange("(k p) -> k p", p=P)),
                (gain_rows[MEM_K:MEM_K + 2, :], io["mem_k_norm"][0].rearrange("(k p) -> k p", p=P)),
                (gain_rows[SB_Q:SB_Q + 1, :], io["sb_q_norm"]),
                (gain_rows[SB_K:SB_K + 1, :], io["sb_k_norm"]),
                (qk_gain[:, 0, :], io["a_q_norm"][0].partition_broadcast(P)),
                (qk_gain[:, 1, :], io["a_k_norm"][0].partition_broadcast(P)),
            ):
                pool.dma_start(dst, src).then_inc(const_in, 16)
                n += 1
            assert n == N_CONST
            pool.wait_ge(gains_free, 1)
            pool.dma_start(qk_gain[:, 0, :], io["b_q_norm"][0].partition_broadcast(P)).then_inc(table_in, 16)
            pool.dma_start(qk_gain[:, 1, :], io["b_k_norm"][0].partition_broadcast(P)).then_inc(table_in, 16)
            pool.wait_ge(xn_kept, 8)
            pool.dma_start(x_mid, x[:]).then_inc(x_kept, 16)
            pool.wait_ge(phase_done, 1)
            pool.dma_start(sq[:], io["c_squares"][:, 1:, :]).then_inc(small_in, 16)
            for t in range(TT):
                pool.dma_start(mem_nat[:, t, :], io["mem"][0, t * P:(t + 1) * P, :]).then_inc(mem_in, 16)
            pool.wait_ge(phase_done, 2)
            pool.dma_start(w_a2[:], io["w_a2"][0]).then_inc(small_in, 16)
            pool.dma_start(b_a[:], io["b_a"][0].partition_broadcast(P)).then_inc(small_in, 16)
            pool.dma_start(g_gain[:], io["gla_norm"][0].partition_broadcast(P)).then_inc(small_in, 16)
            pool.wait_ge(phase_done, 3)
            pool.dma_start(x[:], x_mid).then_inc(x_back, 16)

        @block.scalar
        def _(act):
            c, m, mh = Count(), Count(), Count()
            nb, s_max, s_gate = Count(), Count(), Count()

            def split_hi(d=0):
                k = c.k + d
                act.wait_ge(raw_in[k % RAW], chunk_loads(c, d))
                if k >= SPL:
                    act.wait_ge(chunk_done, c(d + 1 - SPL))
                act.activation(w_hi[:, k % SPL], raw[:, k % RAW], ACT.Copy).then_inc(hi_done, 1)

            def ahead():
                if c.reg is not None or c.k + LEAD < N_CHUNKS:
                    split_hi(LEAD)
                c.step()

            def turned_hi(buf, k0, gain=None):
                act.wait_ge(m_full, m(1))
                src = M[m.k % 2][:].rearrange("p (k t) -> p k t", k=2)
                if gain is None:
                    last = act.activation(a_hi[buf][:, bass.ds(k0, 2), :], src, ACT.Copy)
                else:
                    for i in range(2):
                        last = act.activation(a_hi[buf][:, bass.ds(k0 + i, 1), :], src[:, i:i + 1, :], ACT.Copy,
                                              scale=gains[:, bass.ds(gain * KT + k0 + i, 1)])
                last.then_inc(m_hi, 1)
                m.step()
                mh.step()

            def exps():
                h = s_max.k
                act.wait_ge(max_ready, s_max(1))
                for t in range(TT):
                    cols = slice(t * P, t * P + P * (t + 1))
                    last = act.activation(probs[:, h % 2, cols], probs[:, h % 2, cols], ACT.Exp,
                                          bias=row[:, 1, 2 * (h % HPG) + t:2 * (h % HPG) + t + 1], scale=SCALE,
                                          accum_out=row[:, 2, 2 * (h % HPG) + t:2 * (h % HPG) + t + 1])
                last.then_inc(probs_ready, 1)
                s_max.step()

            def skip_turned(n=1):
                m.step(n)

            split_hi(0)
            split_hi(1)
            act.wait_ge(x_in, 16 * TT)
            for t in range(TT):
                last = act.activation(row_sq[:, t, :], x[:, t, :], ACT.Square, accum_out=ss[:, t:t + 1])
            last.then_inc(squares_ready, 1)
            skip_turned()
            act.wait_ge(m_free, m())
            for h in range(KT // 2):
                turned_hi(0, 2 * h, 0)

            for b in range(5):
                for p in range(4):
                    ahead()
                if b in (1, 3):
                    skip_turned(2)
                if b == 4:
                    skip_turned(3)
                    for h in range(IDX_HEADS):
                        act.wait_ge(m_full, m(1))
                        act.activation(relus[:, h % 2, :], M[m.k % 2][:, 0:W0], ACT.Relu).then_inc(relu_ready, 1)
                        m.step()

            def gate():
                act.wait_ge(gate_ready, s_gate(1))
                act.activation(silu_g[:], silu_g[:], ACT.Silu).then_inc(silu_ready, 1)
                s_gate.step()

            def turn(with_heads, with_blocks, b0):
                for p in range(8):
                    if with_blocks:
                        ahead()
                    if with_heads and p < 4:
                        exps()
                    if with_heads and 1 <= p <= 4:
                        skip_turned()
                    if with_heads and p == 6:
                        turned_hi(1, b0)
                        turned_hi(1, b0 + 2)
                    if with_blocks and p == 6:
                        skip_turned(2)
                    if with_blocks and p == 7:
                        gate()
                        nb.step(2)

            def project_out(nbuf, gain):
                for j in loop(act, 0, 2, {c: 8, nb: 2, m: 4, mh: 4}):
                    for p in range(8):
                        ahead()
                        if p in (5, 7):
                            u = p // 2 - 2
                            act.wait_ge(block_read, nb(1))
                            nb.step()
                            act.activation(x[:, :, bass.ds(j * (2 * NB) + u * NB, NB)], x_new[:, u], ACT.Copy)
                            for t in range(TT):
                                last = act.activation(junk[:, u, t, :], x_new[:, u, t, :], ACT.Square,
                                                      accum_out=ss_part[:, u, t:t + 1])
                            last.then_inc(xn_kept, 1)
                            for i in range(2):
                                turned_hi(nbuf, j * 8 + 4 * u + 2 * i, gain)

            nb.step(5)
            for layer in range(2):
                if layer:
                    for p in range(8):
                        ahead()
                    nb.step(2)
                    skip_turned(2)
                turn(False, True, 0)
                for j in loop(act, 1, GROUPS, {c: 8, nb: 2, m: 8, mh: 2, s_max: 4, s_gate: 1}):
                    turn(True, True, j * 4 - 4)
                turn(True, False, 4 * GROUPS - 4)
                project_out(0, layer + 1)

            s_a, a_q = Count(), Count()

            def seq(ins):
                ins.then_inc(a_seq, 1)
                a_q.step()
                act.wait_ge(a_seq, a_q())

            def asked():
                act.wait_ge(for_act, s_a(1))
                s_a.step()

            def answered(ins):
                ins.then_inc(from_act, 1)

            def blocks(n, per=4):
                for _ in range(n):
                    for _ in range(per):
                        ahead()
                    nb.step()

            def log1p_exp(buf):
                asked()
                seq(act.activation(buf, buf, ACT.Exp))
                answered(act.activation(buf, buf, ACT.Ln, bias=1.0))

            act.wait_ge(mem_in, 16 * TT)
            for t in range(TT):
                last = act.activation(row_sq2[:, t, :], mem_nat[:, t, :], ACT.Square, accum_out=mem_ss[:, t:t + 1])
            answered(last)
            blocks(1)
            for h in range(KT // 2):
                turned_hi(1, 2 * h, 3)
            blocks(1)
            skip_turned(2)
            blocks(1)
            skip_turned(2)
            blocks(1)
            skip_turned(2)
            blocks(1)
            skip_turned(2)
            blocks(1)
            for h in range(MEM_HEADS):
                asked()
                for t in range(TT):
                    last = act.activation(m_probs[:, h % 2, t, :], L[:, t * T:(t + 1) * T], ACT.Exp,
                                          bias=stat[:, 1, t:t + 1], scale=MEM_DH ** -0.5, accum_out=stat[:, 2, t:t + 1])
                answered(last)
                skip_turned()
                turned_hi(1, 2 * h)

            def branch():
                for j in loop(act, 0, 2, {c: 12, nb: 4, s_sig: 2}):
                    for u in range(2):
                        for p in range(6):
                            ahead()
                            if p == 3:
                                act.wait_ge(block_read, nb(1))
                                act.activation(b_gate[:, u], b_gate[:, u], ACT.Sigmoid).then_inc(sig_ready, 1)
                                s_sig.step()
                        nb.step(2)

            s_sig = Count()
            branch()
            blocks(7)
            asked()
            answered(act.activation(gr[:], gr[:], ACT.Silu))
            skip_turned()
            for t in range(TT):
                log1p_exp(e_in[:])
                act.wait_ge(l_full, 4 * GROUPS * 2 + MEM_HEADS + 3 * t + 2)
                seq(act.activation(e_in[:], L[:], ACT.Exp, scale=1 / GLA_TAU))
                seq(act.activation(e_neg[:], L[:], ACT.Exp, scale=-1 / GLA_TAU))
                act.wait_ge(o_full, 4 * GROUPS * 2 + 2 * t + 1)
                seq(act.activation(e_rest[:], O[:], ACT.Exp, scale=1 / GLA_TAU))
                asked()
                answered(act.activation(decay[:, t], decay[:, t], ACT.Exp, scale=1 / GLA_TAU))
                skip_turned(1 + 2 + 1 + 4 - 2 * t)
            for h in range(4):
                turned_hi(1, 2 * h)
            branch()
            blocks(6)
            for pair in range(SB_HEADS // 2):
                for h in range(2):
                    skip_turned()
                    act.wait_ge(l_full, 4 * GROUPS * 2 + MEM_HEADS + 3 * TT + 2 * pair + h + 1)
                    seq(act.activation(soft_p[:, h, :], L[:, 0:W0], ACT.Abs))
                    seq(act.activation(soft_p[:, h, :], soft_p[:, h, :], ACT.Exp, scale=-1.0))
                    answered(act.activation(soft_p[:, h, :], soft_p[:, h, :], ACT.Ln, bias=1.0))
                for h in range(2):
                    asked()
                    answered(act.activation(stick[:, h, :], stick[:, h, :], ACT.Exp))
                turned_hi(1, 2 * pair)
            branch()
            for h in range(KT // 2):
                turned_hi(0, 2 * h)
            project_out(1, 4)
            for b0, n in FF_PARTS:
                def ffn_turn(prev, b):
                    for p in range(8):
                        ahead()
                        if p == 2 and prev:
                            for i in range(2):
                                turned_hi(0, b * 4 - 4 + 2 * i)
                        if p == 3:
                            act.wait_ge(block_read, nb(1))
                            act.activation(f_gate[:], f_gate[:], ACT.Silu).then_inc(sig_ready, 1)
                    nb.step(2)

                ffn_turn(False, 0)
                for j in loop(act, 1, n, {c: 8, nb: 2, m: 2, mh: 2}):
                    ffn_turn(True, j)
                for i in range(2):
                    turned_hi(0, n * 4 - 4 + 2 * i)
                if n == 4:
                    for j in loop(act, 0, 2, {c: 8, nb: 2}):
                        blocks(2)
                else:
                    blocks(4, n)

        @block.vector
        def _(v):
            c, nb, m, mh, l, o, q = Count(), Count(), Count(), Count(), Count(), Count(), Count()
            s_silu, s_relu, s_xn, s_rot = Count(), Count(), Count(), Count()

            def seq(ins):
                ins.then_inc(v_seq, 1)
                q.step()
                v.wait_ge(v_seq, q())

            def split_lo(d=0):
                k = c.k + d
                v.wait_ge(hi_done, c(d + 1))
                v.tensor_tensor(w_lo[:, k % SPL], raw[:, k % RAW], w_hi[:, k % SPL].bitcast(F32),
                                ALU.subtract).then_inc(lo_done, 1)

            def ahead():
                if c.reg is not None or c.k + LEAD < N_CHUNKS:
                    split_lo(LEAD)
                c.step()

            def read_block(dst, width=NB, rows=rstd):
                v.wait_ge(chunk_done, c())
                for t in range(TT):
                    last = v.tensor_scalar(dst[:, t, 0:width], G[nb.k % 2][t][:, 0:width], rows[:, t:t + 1], None,
                                           ALU.mult)
                    if t == TT - 1:
                        last.then_inc(block_read, 1)
                    nb.step(t)
                v.wait_ge(block_read, nb())

            def turned_lo(buf, k0, gain=None):
                v.wait_ge(m_full, m(1))
                v.wait_ge(m_hi, mh(1))
                src = M[m.k % 2][:].rearrange("p (k t) -> p k t", k=2)
                if gain is None:
                    last = v.tensor_tensor(a_lo[buf][:, bass.ds(k0, 2), :], src,
                                           a_hi[buf][:, bass.ds(k0, 2), :].bitcast(F32), ALU.subtract)
                else:
                    for i in range(2):
                        last = v.scalar_tensor_tensor(
                            out=a_lo[buf][:, bass.ds(k0 + i, 1), :], in0=src[:, i:i + 1, :],
                            scalar=gains[:, bass.ds(gain * KT + k0 + i, 1)],
                            in1=a_hi[buf][:, bass.ds(k0 + i, 1), :].bitcast(F32), op0=ALU.mult, op1=ALU.subtract)
                last.then_inc(m_free, 1)
                m.step()
                mh.step()

            def turned_copy(dst):
                v.wait_ge(m_full, m(1))
                v.tensor_copy(dst, M[m.k % 2][:, 0:dst.free_size()]).then_inc(m_free, 1)
                m.step()

            def rsqrt(dst, src, width, n):
                a, y, z = (newton[:, i, 0:n] for i in range(3))
                yi = y.bitcast(I32)
                seq(v.tensor_scalar(a, src, 1.0 / width, EPS, ALU.mult, ALU.add))
                seq(v.tensor_scalar(yi, a.bitcast(I32), 1, None, ALU.arith_shift_right))
                seq(v.tensor_scalar(yi, yi, -1.0, RSQRT_SEED, ALU.mult, ALU.add))
                for step in range(3):
                    seq(v.tensor_tensor(z, y, y, ALU.mult))
                    seq(v.tensor_tensor(z, z, a, ALU.mult))
                    seq(v.tensor_scalar(z, z, -0.5, 1.5, ALU.mult, ALU.add))
                    seq(v.tensor_tensor(dst if step == 2 else y, y, z, ALU.mult))

            def heads_of(ap, hd):
                return ap.rearrange("p t (h d) -> p t h d", d=hd)

            def norm_heads(buf, hd, n, tmp=None, then=None):
                tmp = rope_t[:] if tmp is None else tmp
                seq(v.tensor_tensor(tmp, buf, buf, ALU.mult))
                ms = newton[:, 3, 0:n]
                ms3 = ms.rearrange("p (t h) -> p t h", t=TT)
                seq(v.tensor_reduce(ms3, heads_of(tmp, hd), AX.X, ALU.add))
                rsqrt(ms, ms, hd, n)
                by = ms3[:, :, :, None].to_broadcast([P, TT, n // TT, hd])
                last = v.tensor_tensor(heads_of(buf, hd), heads_of(buf, hd), by, ALU.mult)
                seq(last) if then is None else last.then_inc(then, 1)

            def rotate(dst, src, table, hd):
                n, h = src.shape[2] // hd, hd // 2
                s4, d4 = heads_of(src, hd), heads_of(dst, hd)
                t4 = heads_of(rope_t[:, :, 0:src.shape[2]], hd)
                cos, sin = (table[:, i, :, None, :].to_broadcast([P, TT, n, hd]) for i in range(2))
                v.tensor_tensor(t4, s4, cos, ALU.mult)
                v.tensor_tensor(d4[:, :, :, 0:h], s4[:, :, :, h:hd], sin[:, :, :, 0:h], ALU.mult)
                seq(v.tensor_tensor(d4[:, :, :, h:hd], s4[:, :, :, 0:h], sin[:, :, :, h:hd], ALU.mult))
                v.tensor_tensor(dst, dst, rope_t[:, :, 0:src.shape[2]], ALU.add).then_inc(rot_ready, 1)
                s_rot.step()

            def gain_tables():
                for i, dst in ((0, rope_q), (1, rope_k)):
                    g = qk_gain[:, i, None, :].to_broadcast([P, TT, HD])
                    v.tensor_tensor(dst[:, 0], rope[:, 0], g, ALU.mult)
                    h = HD // 2
                    v.tensor_tensor(dst[:, 1, :, 0:h], rope[:, 1, :, 0:h], g[:, :, h:HD], ALU.mult)
                    last = v.tensor_tensor(dst[:, 1, :, h:HD], rope[:, 1, :, h:HD], g[:, :, 0:h], ALU.mult)
                seq(last)

            def soft(r):
                h = r % 2
                v.wait_ge(l_full, l(1))
                v.memset(row[:, 3, 2 * r:2 * r + 2], 0.0)
                mx, nm = row[:, 0, 2 * r:2 * r + 2], row[:, 1, 2 * r:2 * r + 2]
                for t in range(TT):
                    cols = slice(t * P, t * P + P * (t + 1))
                    last = v.tensor_tensor_reduce(out=probs[:, h, cols], in0=L[:, cols], in1=mask_of()[:, cols], scale=1.0,
                                                  scalar=TAKEN, op0=ALU.add, op1=ALU.max, accum_out=mx[:, t:t + 1])
                last.then_inc(l_free, 1)
                l.step()
                v.wait_ge(l_free, l())
                v.tensor_scalar(nm, mx, -SCALE, None, ALU.mult).then_inc(max_ready, 1)

            def weigh(r):
                v.wait_ge(o_full, o(1))
                seq(v.reciprocal(row[:, 3, 2 * r:2 * r + 2], row[:, 2, 2 * r:2 * r + 2]))
                if r == 0:
                    v.wait_ge(silu_ready, s_silu(1))
                    s_silu.step()
                for t in range(TT):
                    last = v.scalar_tensor_tensor(
                        out=o_gated[:, t, r * HD:(r + 1) * HD], in0=O[:, (r % 2) * T + t * P:(r % 2) * T + (t + 1) * P],
                        scalar=row[:, 3, 2 * r + t:2 * r + t + 1], in1=silu_g[:, t, r * HD:(r + 1) * HD],
                        op0=ALU.mult, op1=ALU.mult)
                last.then_inc(o_free, 1)
                o.step()

            masks = [cmask]

            def mask_of():
                return masks[0]

            def turn(with_heads, with_blocks, b0):
                for p in range(8):
                    if with_blocks:
                        ahead()
                    if with_heads:
                        if p < 4:
                            soft(p)
                        if 1 <= p <= 4:
                            turned_copy(probsT[:, (p - 1) % 2, :])
                        if 2 <= p <= 5:
                            weigh(p - 2)
                    if with_blocks and p == 4:
                        read_query()
                    if with_blocks and p == 5:
                        rotate(rot[:], proj[:], rope_q, HD)
                    if with_heads and p == 6:
                        turned_lo(1, b0)
                        turned_lo(1, b0 + 2)
                    if with_blocks and p == 6:
                        for i in range(2):
                            turned_copy(qT[:, 2 * i:2 * i + 2, :].rearrange("p h t -> p (h t)"))
                    if with_blocks and p == 7:
                        read_gate()

            def read_query():
                v.wait_ge(chunk_done, c(-1))
                for t in range(TT):
                    last = v.tensor_scalar(proj[:, t, :], G[nb.k % 2][t][:], rstd[:, t:t + 1], None, ALU.mult)
                last.then_inc(block_read, 1)
                nb.step()
                v.wait_ge(block_read, nb())
                norm_heads(proj[:], HD, TT * HPG)

            def read_gate():
                v.wait_ge(chunk_done, c())
                for t in range(TT):
                    last = v.tensor_scalar(silu_g[:, t, :], G[nb.k % 2][t][:], rstd[:, t:t + 1], None, ALU.mult)
                last.then_inc(block_read, 1)
                nb.step()
                v.wait_ge(block_read, nb())
                v.tensor_scalar(ss_part[:, 0, 0:1], ss_part[:, 0, 0:1], 1.0, None, ALU.mult).then_inc(gate_ready, 1)

            def project_out(nbuf, gain, back=False):
                if back:
                    v.wait_ge(x_back, 16)
                seq(v.memset(ss[:], 0.0))
                for j in loop(v, 0, 2, {c: 8, nb: 2, m: 4, mh: 4, s_xn: 2, q: 2}):
                    for p in range(8):
                        ahead()
                        if p in (3, 7):
                            u = p // 4
                            v.wait_ge(chunk_done, c())
                            for t in range(TT):
                                last = v.tensor_tensor(x_new[:, u, t, :], G[nb.k % 2][t][:],
                                                       x[:, t, bass.ds(j * (2 * NB) + u * NB, NB)], ALU.add)
                            last.then_inc(block_read, 1)
                            nb.step()
                        if p in (5, 7):
                            u = p // 2 - 2
                            v.wait_ge(xn_kept, s_xn(1))
                            s_xn.step()
                            seq(v.tensor_tensor(ss[:], ss[:], ss_part[:, u, :], ALU.add))
                            for i in range(2):
                                turned_lo(nbuf, j * 8 + 4 * u + 2 * i, gain)
                rsqrt(rstd[:], ss[:], D, TT)

            v.memset(ss_part[:], 0.0)
            split_lo(0)
            split_lo(1)
            v.wait_ge(const_in, 16 * N_CONST)
            gain_tables()
            v.tensor_copy(newton[:, 3, 15:16], ident[:, 0:1]).then_inc(gains_free, 1)
            v.wait_ge(squares_ready, 1)
            rsqrt(rstd[:], ss[:], D, TT)
            turned_copy(gains[:])
            for h in range(KT // 2):
                turned_lo(0, 2 * h, 0)

            for _ in range(4):
                ahead()
            read_block(proj)
            norm_heads(proj[:], HD, TT * HPG)
            rotate(rot[:], proj[:], rope_k, HD)
            for _ in range(4):
                ahead()
            read_block(v_nat)
            for i in range(2):
                turned_copy(kT[:, 2 * i:2 * i + 2, :].rearrange("p h t -> p (h t)"))
            for _ in range(4):
                ahead()
            read_block(proj)
            rotate(rot[:], proj[:], rope64, IDX_DIM)
            for _ in range(4):
                ahead()
            for i in range(2):
                turned_copy(qiT[:, 2 * i:2 * i + 2, :].rearrange("p h t -> p (h t)"))
            read_block(proj)
            rotate(rot[:], proj[:], rope64, IDX_DIM)
            for _ in range(4):
                ahead()
            for i in range(2):
                turned_copy(qiT[:, 4 + 2 * i:6 + 2 * i, :].rearrange("p h t -> p (h t)"))
            read_block(proj, width=80)
            v.tensor_scalar(wi[:], proj[:, :, IDX_DIM:80], IDX_HEADS ** -0.5 * IDX_DIM ** -0.5, None, ALU.mult)
            rotate(ki2[:, :, 0:IDX_DIM], proj[:, :, 0:IDX_DIM], rope64, IDX_DIM)
            v.wait_ge(rot_ready, s_rot())
            v.tensor_copy(ki2[:, :, IDX_DIM:P], ki2[:, :, 0:IDX_DIM]).then_inc(rot_ready, 1)
            s_rot.step()
            turned_copy(kiT[:])
            for h in range(IDX_HEADS):
                v.wait_ge(relu_ready, s_relu(1))
                s_relu.step()
                prev = cmask if h == 0 else score
                for t in range(TT):
                    cols = slice(t * P, t * P + P * (t + 1))
                    last = v.scalar_tensor_tensor(out=score[:, cols], in0=relus[:, h % 2, cols], scalar=wi[:, t, h:h + 1],
                                                  in1=prev[:, cols], op0=ALU.mult, op1=ALU.add)
                last.then_inc(m_free, 1)
                m.step()
                v.wait_ge(m_free, m())
            for t in range(TT):
                cols = slice(t * P, t * P + P * (t + 1))
                for _ in range(N_KEEP // 8):
                    seq(v.max(top8[:], score[:, cols]))
                    seq(v.match_replace(score[:, cols], top8[:], score[:, cols], TAKEN))
            seq(v.tensor_scalar(score[:], score[:], TAKEN / 2, NEG, ALU.is_gt, ALU.mult))
            seq(v.tensor_tensor(sel_mask[:], score[:], cmask[:], ALU.add))

            for layer in range(2):
                masks[0] = (sel_mask, cmask)[layer]
                if layer:
                    v.wait_ge(table_in, 32)
                    gain_tables()
                    for _ in range(4):
                        ahead()
                    read_block(proj)
                    norm_heads(proj[:], HD, TT * HPG)
                    rotate(rot[:], proj[:], rope_k, HD)
                    for _ in range(4):
                        ahead()
                    read_block(v_nat)
                    for i in range(2):
                        turned_copy(kT[:, 2 * i:2 * i + 2, :].rearrange("p h t -> p (h t)"))
                turn(False, True, 0)
                for j in loop(v, 1, GROUPS, {c: 8, nb: 2, m: 8, mh: 2, l: 4, o: 4, s_silu: 1, s_rot: 1, q: 23}):
                    turn(True, True, j * 4 - 4)
                turn(True, False, 4 * GROUPS - 4)
                project_out(0, layer + 1)

            s_a, s_sig = Count(), Count()

            def ask(ins):
                ins.then_inc(for_act, 1)

            def answer():
                s_a.step()
                v.wait_ge(from_act, s_a())

            def block_of(dst, width=NB, rows=rstd):
                for _ in range(4):
                    ahead()
                read_block(dst, width, rows)

            def turned_scaled(dst, cols):
                v.wait_ge(m_full, m(1))
                src = M[m.k % 2][:].rearrange("p (k t) -> p k t", k=2)
                for i in range(2):
                    last = v.tensor_scalar(dst[:, i, :], src[:, i, :], cols[i], None, ALU.mult)
                last.then_inc(m_free, 1)
                m.step()

            def gain_cols(first):
                return [gains[:, first + i:first + i + 1] for i in range(2)]

            v.tensor_copy(newton[:, 3, 14:15], ident[:, 0:1]).then_inc(phase_done, 1)
            v.wait_ge(x_kept, 16)
            block_of(pre_q[:])
            answer()
            rsqrt(mem_rstd[:], mem_ss[:], D, TT)
            for h in range(KT // 2):
                turned_lo(1, 2 * h, 3)
            norm_heads(pre_q[:], MEM_DH, 2 * TT, pre_t[:], for_pe)
            block_of(pre[:])
            for i in range(2):
                turned_scaled(mqT[:, 2 * i:2 * i + 2, :], gain_cols(MEM_Q))
            norm_heads(pre[:], MEM_DH, 2 * TT, pre_t[:], for_pe)
            for b in range(2):
                for _ in range(4):
                    ahead()
                for i in range(2):
                    if b == 0:
                        turned_scaled(mqT[:, 4 + 2 * i:6 + 2 * i, :], gain_cols(MEM_Q))
                    else:
                        turned_scaled(mkT[:, 2 * i:2 * i + 2, :], gain_cols(MEM_K))
                read_block(pre[:], rows=mem_rstd)
                norm_heads(pre[:], MEM_DH, 2 * TT, pre_t[:], for_pe)
            block_of(mv[:, :, 0:NB], rows=mem_rstd)
            for i in range(2):
                turned_scaled(mkT[:, 4 + 2 * i:6 + 2 * i, :], gain_cols(MEM_K))
            block_of(mv[:, :, NB:2 * NB], rows=mem_rstd)
            for h in range(MEM_HEADS):
                v.wait_ge(l_full, l(1))
                l.step()
                seq(v.tensor_reduce(stat[:, 0, 0:2], L[:].rearrange("p (t m) -> p t m", t=TT), AX.X, ALU.max))
                ask(v.tensor_scalar(stat[:, 1, 0:2], stat[:, 0, 0:2], -MEM_DH ** -0.5, None, ALU.mult))
                answer()
                seq(v.reciprocal(stat[:, 3, 0:2], stat[:, 2, 0:2]))
                for t in range(TT):
                    last = v.tensor_scalar(m_probs[:, h % 2, t, :], m_probs[:, h % 2, t, :], stat[:, 3, t:t + 1], None,
                                           ALU.mult)
                last.then_inc(l_free, 1)
                turned_copy(m_probsT[:, h % 2].rearrange("p s t -> p (s t)"))
                turned_lo(1, 2 * h)

            def branch(first):
                for j in loop(v, 0, 2, {c: 12, nb: 4, s_sig: 2, q: 0 if first else 2}):
                    for u in range(2):
                        for p in range(6):
                            ahead()
                            if p == 3:
                                v.wait_ge(chunk_done, c())
                                for t in range(TT):
                                    last = v.tensor_scalar(b_gate[:, u, t, :], G[nb.k % 2][t][:], rstd[:, t:t + 1], None,
                                                           ALU.mult)
                                last.then_inc(block_read, 1)
                                nb.step()
                        v.wait_ge(sig_ready, s_sig(1))
                        s_sig.step()
                        v.wait_ge(chunk_done, c())
                        at_col = bass.ds(j * (2 * NB) + u * NB, NB)
                        for t in range(TT):
                            dst = x[:, t, at_col] if first else b_tmp[:, t, :]
                            last = v.tensor_tensor(dst, G[nb.k % 2][t][:], b_gate[:, u, t, :], ALU.mult)
                        last.then_inc(block_read, 1)
                        nb.step()
                        if not first:
                            v.wait_ge(block_read, nb())
                            seq(v.tensor_tensor(x[:, :, at_col], x[:, :, at_col], b_tmp[:], ALU.add))

            v.tensor_copy(stat[:, 0, 4:5], stat[:, 0, 0:1]).then_inc(phase_done, 1)
            branch(True)
            block_of(gq[:])
            block_of(gk[:])
            for b in range(2):
                block_of(gv[:, :, b * NB:(b + 1) * NB])
            for b in range(2):
                block_of(gr[:, :, b * NB:(b + 1) * NB])
            for _ in range(4):
                ahead()
            read_block(ga[:], width=16)
            ask(v.tensor_copy(stat2[:], ga[:, 0, 0:1]))
            v.wait_ge(m_full, m(1))
            v.tensor_copy(gaT[:], M[m.k % 2][0:16, 0:T]).then_inc(m_free, 1)
            m.step()
            v.wait_ge(small_in, 64)
            for t in range(TT):
                v.wait_ge(l_full, l(1))
                l.step()
                v.tensor_tensor(log_a[:], L[:], b_a[:], ALU.add).then_inc(l_free, 1)
                v.wait_ge(l_free, l())
                if t == 0:
                    answer()
                ask(v.scalar_tensor_tensor(out=e_in[:], in0=log_a[:], scalar=-1.0, in1=log_a[:], op0=ALU.mult, op1=ALU.min))
                answer()
                v.scalar_tensor_tensor(out=log_a[:], in0=log_a[:], scalar=0.0, in1=e_in[:], op0=ALU.min,
                                       op1=ALU.subtract).then_inc(for_pe, 1)
                v.wait_ge(m_full, m(1))
                ask(v.tensor_copy(decay[:, t].rearrange("p h e -> p (h e)"), M[m.k % 2][:, 0:2 * GLA_HEADS]))
                answer()
                v.tensor_scalar(decay2[:], stat2[:], 1.0, None, ALU.mult).then_inc(m_free, 1)
                m.step()
                v.wait_ge(l_full, l(1))
                v.wait_ge(o_full, o(1))
                v.scalar_tensor_tensor(out=gq[:, t, :], in0=gq[:, t, :], scalar=GLA_DK ** -0.5, in1=e_in[:],
                                       op0=ALU.mult, op1=ALU.mult).then_inc(l_free, 1)
                l.step()
                v.tensor_tensor(kd[:], gk[:, t, :], e_rest[:], ALU.mult).then_inc(o_free, 1)
                o.step()
                v.tensor_tensor(gk[:, t, :], gk[:, t, :], e_neg[:], ALU.mult).then_inc(for_pe, 1)
                turned_copy(qeT[:])
                turned_copy(keT[:])
                v.wait_ge(m_full, m(1))
                s4 = sT[:].rearrange("p (h t) -> p h t", h=GLA_HEADS)
                bound = [b[:, None, :].to_broadcast([P, GLA_HEADS, P]) for b in (at_most, at_least)]
                v.tensor_tensor(s4, M[m.k % 2][:].rearrange("p (h t) -> p h t", h=GLA_HEADS), bound[0],
                                ALU.min).then_inc(m_free, 1)
                m.step()
                v.wait_ge(m_free, m())
                v.tensor_tensor(s4, s4, bound[1], ALU.max).then_inc(for_pe, 1)
                for half in range(2):
                    n = 2 * t + half
                    if n == 3:
                        continue
                    for pair in range(2):
                        v.wait_ge(m_full, m(1))
                        for i in range(2):
                            h, src = 2 * pair + i, M[m.k % 2][:, i * GLA_DV:(i + 1) * GLA_DV]
                            if n == 0:
                                last = v.tensor_copy(state[:, h, :], src)
                            else:
                                last = v.scalar_tensor_tensor(out=state[:, h, :], in0=state[:, h, :],
                                                              scalar=decay[:, t, h, half:half + 1], in1=src,
                                                              op0=ALU.mult, op1=ALU.add)
                        last.then_inc(m_free, 1)
                        m.step()
                        v.wait_ge(m_free, m())
                v.wait_ge(l_full, l(1))
                v.wait_ge(o_full, o(1))
                v.tensor_copy(g_out[:, 0:2, :].rearrange("p h d -> p (h d)"), L[:]).then_inc(l_free, 1)
                v.tensor_copy(g_out[:, 2:4, :].rearrange("p h d -> p (h d)"), O[:]).then_inc(o_free, 1)
                l.step()
                o.step()
                v.wait_ge(l_free, l())
                v.wait_ge(o_free, o())
                seq(v.tensor_tensor(g_sq[:], g_out[:], g_out[:], ALU.mult))
                ms = newton[:, 3, 0:GLA_HEADS]
                seq(v.tensor_reduce(ms, g_sq[:], AX.X, ALU.add))
                rsqrt(ms, ms, GLA_DV, GLA_HEADS)
                seq(v.tensor_tensor(g_out[:], g_out[:], ms[:, :, None].to_broadcast([P, GLA_HEADS, GLA_DV]), ALU.mult))
                seq(v.tensor_tensor(g_out[:], g_out[:], g_gain[:, None, :].to_broadcast([P, GLA_HEADS, GLA_DV]), ALU.mult))
                gr4 = gr[:, t, :].rearrange("p (h d) -> p h d", h=GLA_HEADS)
                v.tensor_tensor(gr4, gr4, g_out[:], ALU.mult).then_inc(for_pe, 1)
            for h in range(4):
                turned_lo(1, 2 * h)
            branch(False)
            v.tensor_scalar(sb_gain[:, 0:1], gains[:, SB_Q:SB_Q + 1], HD ** -0.5, None, ALU.mult)
            seq(v.tensor_copy(sb_gain[:, 1:2], gains[:, SB_K:SB_K + 1]))
            for nat in (sq_nat, sk_nat):
                for b in range(2):
                    block_of(nat[:, :, b * NB:(b + 1) * NB])
                    norm_heads(nat[:, :, b * NB:(b + 1) * NB], HD, TT * 4, sb_tmp[:])
            for b in range(2):
                block_of(sv_nat[:, :, b * NB:(b + 1) * NB])
            v.tensor_copy(stat3[:], ident[:, 0:1]).then_inc(for_pe, 1)
            for pair in range(SB_HEADS // 2):
                for h in range(2):
                    turned_scaled(qkT[:, h], [sb_gain[:, 0:1], sb_gain[:, 1:2]])
                    v.wait_ge(l_full, l(1))
                    l.step()
                    answer()
                    v.scalar_tensor_tensor(out=stick[:, h, :], in0=L[:, 0:W0], scalar=0.0, in1=soft_p[:, h, :],
                                           op0=ALU.min, op1=ALU.subtract)
                    v.scalar_tensor_tensor(out=neg_l[:, h, :], in0=L[:, 0:W0], scalar=0.0, in1=soft_p[:, h, :],
                                           op0=ALU.max, op1=ALU.add).then_inc(l_free, 1)
                    v.wait_ge(l_free, l())
                    diag = neg_l[:, h, :].rearrange("p (b t) -> p b t", b=3)[:, 0:3:2, :]
                    v.tensor_tensor(diag, diag, strict[:, None, :].to_broadcast([P, 2, P]), ALU.mult).then_inc(for_pe, 1)
                for h in range(2):
                    v.wait_ge(o_full, o(1))
                    o.step()
                    v.tensor_tensor(stick[:, h, :], stick[:, h, :], O[:, 0:W0], ALU.subtract).then_inc(o_free, 1)
                    v.wait_ge(o_free, o())
                    ask(v.tensor_copy(stat3[:], ident[:, 0:1]))
                    answer()
                    diag = stick[:, h, :].rearrange("p (b t) -> p b t", b=3)[:, 0:3:2, :]
                    v.tensor_tensor(diag, diag, strict[:, None, :].to_broadcast([P, 2, P]), ALU.mult).then_inc(for_pe, 1)
                turned_lo(1, 2 * pair)
            branch(False)
            v.tensor_copy(stat3[:], ident[:, 0:1]).then_inc(for_pe, 1)
            for h in range(KT // 2):
                turned_lo(0, 2 * h)
            v.wait_ge(m_free, m())
            v.tensor_copy(stat4[:], ident[:, 0:1]).then_inc(phase_done, 1)
            project_out(1, 4, True)
            for b0, n in FF_PARTS:
                def ffn_turn(prev, b):
                    for p in range(8):
                        ahead()
                        if p == 2 and prev:
                            for i in range(2):
                                turned_lo(0, b * 4 - 4 + 2 * i)
                        if p == 3:
                            v.wait_ge(chunk_done, c())
                            for t in range(TT):
                                last = v.tensor_scalar(f_gate[:, t, :], G[nb.k % 2][t][:], rstd[:, t:t + 1], None, ALU.mult)
                            last.then_inc(block_read, 1)
                            nb.step()
                        if p == 7:
                            v.wait_ge(chunk_done, c())
                            v.wait_ge(sig_ready, s_sig(1))
                            s_sig.step()
                            for t in range(TT):
                                last = v.scalar_tensor_tensor(out=f_mid[:, t, :], in0=G[nb.k % 2][t][:],
                                                              scalar=rstd[:, t:t + 1], in1=f_gate[:, t, :],
                                                              op0=ALU.mult, op1=ALU.mult)
                            last.then_inc(block_read, 1)
                            nb.step()

                def add_down(b, chunks, done=block_read):
                    for _ in range(chunks):
                        ahead()
                    v.wait_ge(chunk_done, c())
                    for t in range(TT):
                        dst = x[:, t, bass.ds(b * NB, NB)]
                        last = v.tensor_tensor(dst, G[nb.k % 2][t][:], dst, ALU.add)
                    last.then_inc(done, 1)
                    nb.step()

                ffn_turn(False, 0)
                for j in loop(v, 1, n, {c: 8, nb: 2, m: 2, mh: 2, s_sig: 1}):
                    ffn_turn(True, j)
                for i in range(2):
                    turned_lo(0, n * 4 - 4 + 2 * i)
                if n == 4:
                    for j in loop(v, 0, 2, {c: 8, nb: 2}):
                        for u in range(2):
                            add_down(j * 2 + u, 4)
                else:
                    for b in range(4):
                        add_down(b, n, block_read if b < 2 else x_final)
                        if b < 2:
                            v.wait_ge(block_read, nb())
                            v.tensor_copy(stat4[:], ident[:, 0:1]).then_inc(x_final, 1)

        @block.tensor
        def _(pe):
            c, nb, m, l, o = Count(), Count(), Count(), Count(), Count()
            s_rot, s_probs = Count(), Count()

            def chunk(buf, kc, n_kc, bank2, width=NB):
                s = c.k % SPL
                pe.wait_ge(lo_done, c(1))
                for t in range(TT):
                    toks = slice(t * P, (t + 1) * P)
                    for i in range(KC):
                        k = kc * KC + i
                        dst = bank2[t][:, 0:width]
                        xh, xl = a_hi[buf][:, k, toks], a_lo[buf][:, k, toks]
                        wh, wl = w_hi[:, s, i, 0:width], w_lo[:, s, i, 0:width]
                        pe.matmul(dst, xh, wh, start=(k == 0), stop=False)
                        pe.matmul(dst, xh, wl, start=False, stop=False)
                        last = pe.matmul(dst, xl, wh, start=False, stop=(k == n_kc * KC - 1))
                last.then_inc(chunk_done, 1)
                c.step()

            def bank_for_block():
                if nb.k >= 2:
                    pe.wait_ge(block_read, nb(-1))
                nb.step()
                return G[(nb.k - 1) % 2]

            def gemm(buf, n_kc=KT // KC, width=NB):
                dst = bank_for_block()
                for kc in range(n_kc):
                    chunk(buf, kc, n_kc, dst, width)

            def turned_bank():
                if m.k >= 2:
                    pe.wait_ge(m_free, m(-1))
                m.step()
                return M[(m.k - 1) % 2]

            def turn_two(src, f0):
                dst = turned_bank()
                for i in range(2):
                    for t in range(TT):
                        last = pe.transpose(dst[:, i * T + t * P:i * T + (t + 1) * P],
                                            src[:, t, (f0 + i) * P:(f0 + i + 1) * P], ident)
                last.then_inc(m_full, 1)

            def turn_rot(n=4):
                pe.wait_ge(rot_ready, s_rot(1))
                s_rot.step()
                for i in range(0, n, 2):
                    turn_two(rot, i)

            def logits(r, g):
                if l.k >= 1:
                    pe.wait_ge(l_free, l())
                if r == 0:
                    pe.wait_ge(m_free, m())
                for t in range(TT):
                    last = pe.matmul(L[:, t * P:t * P + P * (t + 1)], qT[:, r, t * P:(t + 1) * P],
                                     kT[:, bass.ds(g, 1), 0:P * (t + 1)].rearrange("p a t -> p (a t)"),
                                     start=True, stop=True)
                last.then_inc(l_full, 1)
                l.step()

            def turn_probs(r):
                pe.wait_ge(probs_ready, s_probs(1))
                s_probs.step()
                dst = turned_bank()
                for i in range(3):
                    last = pe.transpose(dst[:, i * P:(i + 1) * P], probs[:, r % 2, i * P:(i + 1) * P], ident)
                last.then_inc(m_full, 1)

            def mix(r, g, later):
                pe.wait_ge(m_free, m(-later))
                if o.k >= 1:
                    pe.wait_ge(o_free, o())
                at0 = (r % 2) * T
                val = [v_nat[:, s, bass.ds(g * HD, HD)] for s in range(TT)]
                pe.matmul(O[:, at0:at0 + P], probsT[:, r % 2, 0:P], val[0], start=True, stop=True)
                pe.matmul(O[:, at0 + P:at0 + T], probsT[:, r % 2, P:2 * P], val[0], start=True, stop=False)
                pe.matmul(O[:, at0 + P:at0 + T], probsT[:, r % 2, 2 * P:3 * P], val[1], start=False,
                          stop=True).then_inc(o_full, 1)
                o.step()

            def turn(with_heads, with_blocks, g):
                for p in range(8):
                    if with_blocks:
                        if p % 4 == 0:
                            dst = bank_for_block()
                        chunk(0, p % 4, 4, dst)
                    if with_heads:
                        if p < 4:
                            logits(p, g)
                        if 1 <= p <= 4:
                            turn_probs(p - 1)
                        if 2 <= p <= 5:
                            mix(p - 2, g, 0 if p == 5 else 1)
                        if p == 6:
                            pe.wait_ge(o_free, o())
                            turn_two(o_gated, 0)
                            turn_two(o_gated, 2)
                    if with_blocks and p == 6:
                        turn_rot()

            def project_out(src):
                pe.wait_ge(m_free, m())
                for j in loop(pe, 0, 2, {c: 8, nb: 2, m: 4}):
                    for p in range(8):
                        if p % 4 == 0:
                            dst = bank_for_block()
                        chunk(src, p % 4, 4, dst)
                        if p in (5, 7):
                            u = p // 2 - 2
                            pe.wait_ge(block_read, nb(u - 1))
                            turn_two(x_new[:, u], 0)
                            turn_two(x_new[:, u], 2)

            pe.wait_ge(const_in, 16 * N_CONST)
            pe.transpose(turned_bank()[:, 0:N_GAINS], gain_rows[:], ident[0:N_GAINS, 0:N_GAINS]).then_inc(m_full, 1)
            pe.wait_ge(x_in, 16 * TT)
            for h in range(KT // 2):
                turn_two(x, 2 * h)
            pe.wait_ge(m_free, m())
            gemm(0)
            gemm(0)
            turn_rot()
            gemm(0)
            gemm(0)
            turn_rot()
            gemm(0, width=80)
            turn_rot()
            pe.wait_ge(rot_ready, s_rot(2))
            s_rot.step(2)
            dst = turned_bank()
            for t in range(TT):
                last = pe.transpose(dst[:, t * P:(t + 1) * P], ki2[:, t, :], ident)
            last.then_inc(m_full, 1)
            pe.wait_ge(m_free, m())
            for h in range(IDX_HEADS):
                dst = turned_bank()
                side = slice(IDX_DIM * (h % 2), IDX_DIM * (h % 2) + IDX_DIM)
                for t in range(TT):
                    last = pe.matmul(dst[:, t * P:t * P + P * (t + 1)], qiT[side, h // 2, t * P:(t + 1) * P],
                                     kiT[side, 0:P * (t + 1)], start=True, stop=True)
                last.then_inc(m_full, 1)
            for layer in range(2):
                if layer:
                    pe.wait_ge(m_free, m())
                    gemm(0)
                    gemm(0)
                    turn_rot()
                turn(False, True, 0)
                for j in loop(pe, 1, GROUPS, {c: 8, nb: 2, m: 8, l: 4, o: 4, s_rot: 1, s_probs: 4}):
                    turn(True, True, j - 1)
                turn(True, False, GROUPS - 1)
                project_out(1)

            s_op = Count()

            def operand():
                pe.wait_ge(for_pe, s_op(1))
                s_op.step()

            def turn_all(src, n):
                for h in range(n // 2):
                    turn_two(src, 2 * h)

            gemm(0)
            pe.wait_ge(mem_in, 16 * TT)
            turn_all(mem_nat, KT)
            gemm(0)
            operand()
            turn_all(pre_q, 4)
            for b in range(4):
                pe.wait_ge(m_free, m(-2 if b == 0 else 0) if b == 0 else m())
                gemm(1)
                if b < 3:
                    operand()
                    turn_all(pre, 4)
            pe.wait_ge(m_free, m())
            pe.wait_ge(block_read, nb())
            for h in range(MEM_HEADS):
                pe.wait_ge(l_free, l())
                for t in range(TT):
                    for e in range(2):
                        last = pe.matmul(L[:, t * T:(t + 1) * T], mqT[:, 2 * h + e, t * P:(t + 1) * P], mkT[:, 2 * h + e, :],
                                         start=(e == 0), stop=(e == 1))
                last.then_inc(l_full, 1)
                l.step()
                pe.wait_ge(l_free, l())
                dst = turned_bank()
                for s in range(2):
                    for t in range(TT):
                        last = pe.transpose(dst[:, s * T + t * P:s * T + (t + 1) * P],
                                            m_probs[:, h % 2, t, s * P:(s + 1) * P], ident)
                last.then_inc(m_full, 1)
                pe.wait_ge(m_free, m())
                dst = turned_bank()
                for e in range(2):
                    for s in range(2):
                        last = pe.matmul(dst[:, e * T:(e + 1) * T], mv[:, s, h * MEM_DH + e * P:h * MEM_DH + (e + 1) * P],
                                         m_probsT[:, h % 2, s, :], start=(s == 0), stop=(s == 1))
                last.then_inc(m_full, 1)

            def branch():
                pe.wait_ge(m_free, m())
                for j in loop(pe, 0, 2, {c: 12, nb: 4}):
                    for u in range(2):
                        gemm(0)
                        gemm(1, MIX_KC)

            branch()
            for b in range(6):
                gemm(0)
            gemm(0, width=16)
            pe.wait_ge(block_read, nb())
            dst = turned_bank()
            for t in range(TT):
                last = pe.transpose(dst[0:16, t * P:(t + 1) * P], ga[:, t, :], ident)
            last.then_inc(m_full, 1)
            pe.wait_ge(m_free, m())
            pe.wait_ge(small_in, 64)
            for t in range(TT):
                pe.wait_ge(l_free, l())
                pe.matmul(L[:], gaT[:, t * P:(t + 1) * P], w_a2[:], start=True, stop=True).then_inc(l_full, 1)
                l.step()
                operand()
                dst = turned_bank()
                for h in range(GLA_HEADS):
                    last = pe.matmul(dst[:, 2 * h:2 * h + 2], log_a[:, h * P:(h + 1) * P], ends[:], start=True, stop=True)
                last.then_inc(m_full, 1)
                pe.wait_ge(l_free, l())
                pe.matmul(L[:], cum64, log_a[:], start=True, stop=True).then_inc(l_full, 1)
                l.step()
                pe.wait_ge(o_free, o())
                pe.matmul(O[:], after64, log_a[:], start=True, stop=True).then_inc(o_full, 1)
                o.step()
                operand()
                for nat in (gq, gk):
                    dst = turned_bank()
                    for h in range(GLA_HEADS):
                        last = pe.transpose(dst[:, h * P:(h + 1) * P], nat[:, t, h * P:(h + 1) * P], ident)
                    last.then_inc(m_full, 1)
                pe.wait_ge(m_free, m())
                dst = turned_bank()
                for h in range(GLA_HEADS):
                    last = pe.matmul(dst[:, h * P:(h + 1) * P], keT[:, h * P:(h + 1) * P], qeT[:, h * P:(h + 1) * P],
                                     start=True, stop=True)
                last.then_inc(m_full, 1)
                operand()
                pe.wait_ge(l_free, l())
                pe.wait_ge(o_free, o())
                for half in range(2):
                    n = 2 * t + half
                    rows = slice(half * GLA_CHUNK, (half + 1) * GLA_CHUNK)
                    if n:
                        pe.wait_ge(m_free, m())
                    for h in range(GLA_HEADS):
                        dst = (L, O)[h // 2][rows, (h % 2) * GLA_DV:(h % 2 + 1) * GLA_DV]
                        last = pe.matmul(dst, sT[rows, h * P + half * GLA_CHUNK:h * P + (half + 1) * GLA_CHUNK],
                                         gv[rows, t, h * GLA_DV:(h + 1) * GLA_DV], start=True, stop=(n == 0))
                        if n:
                            last = pe.matmul(dst, qeT[:, h * P + half * GLA_CHUNK:h * P + (half + 1) * GLA_CHUNK],
                                             state[:, h, :], start=False, stop=True)
                        if half and h % 2:
                            last.then_inc((l_full, o_full)[h // 2], 1)
                    if n < 3:
                        for pair in range(2):
                            dst = turned_bank()
                            for i in range(2):
                                h = 2 * pair + i
                                last = pe.matmul(dst[:, i * GLA_DV:(i + 1) * GLA_DV], kd[rows, h * P:(h + 1) * P],
                                                 gv[rows, t, h * GLA_DV:(h + 1) * GLA_DV], start=True, stop=True)
                            last.then_inc(m_full, 1)
                l.step()
                o.step()
                operand()
            turn_all(gr, 8)
            branch()
            for b in range(6):
                gemm(0)
            operand()
            for pair in range(SB_HEADS // 2):
                for i in range(2):
                    h = 2 * pair + i
                    dst = turned_bank()
                    for n, nat in enumerate((sq_nat, sk_nat)):
                        for t in range(TT):
                            last = pe.transpose(dst[:, n * T + t * P:n * T + (t + 1) * P], nat[:, t, h * P:(h + 1) * P], ident)
                    last.then_inc(m_full, 1)
                    pe.wait_ge(m_free, m())
                    pe.wait_ge(l_free, l())
                    pe.matmul(L[:, 0:T], qkT[:, i, 1, 0:P], qkT[:, i, 0, :], start=True, stop=True)
                    pe.matmul(L[:, T:W0], qkT[:, i, 1, P:T], qkT[:, i, 0, P:T], start=True, stop=True).then_inc(l_full, 1)
                    l.step()
                for i in range(2):
                    operand()
                    pe.wait_ge(o_free, o())
                    pe.matmul(O[:, 0:W0], after, neg_l[:, i, :], start=True, stop=False)
                    pe.matmul(O[:, P:T], ones, neg_l[:, i, T:W0], start=False, stop=True).then_inc(o_full, 1)
                    o.step()
                dst = turned_bank()
                for i in range(2):
                    h = 2 * pair + i
                    operand()
                    pe.matmul(dst[:, i * T:(i + 1) * T], sv_nat[:, 0, h * P:(h + 1) * P], stick[:, i, 0:T],
                              start=True, stop=False)
                    last = pe.matmul(dst[:, i * T + P:(i + 1) * T], sv_nat[:, 1, h * P:(h + 1) * P], stick[:, i, T:W0],
                                     start=False, stop=True)
                last.then_inc(m_full, 1)
            branch()
            operand()
            turn_all(x, KT)
            project_out(0)
            for b0, n in FF_PARTS:
                def ffn_turn(prev):
                    for p in range(8):
                        if p % 4 == 0:
                            dst = bank_for_block()
                        chunk(1, p % 4, 4, dst)
                        if p == 2 and prev:
                            turn_mid(-1)

                def turn_mid(back):
                    pe.wait_ge(block_read, nb(back))
                    turn_all(f_mid, 4)

                pe.wait_ge(m_free, m())
                ffn_turn(False)
                for j in loop(pe, 1, n, {c: 8, nb: 2, m: 2}):
                    ffn_turn(True)
                turn_mid(0)
                pe.wait_ge(m_free, m())
                if n == 4:
                    for j in loop(pe, 0, 2, {c: 8, nb: 2}):
                        for u in range(2):
                            gemm(0)
                else:
                    for b in range(4):
                        gemm(0, n)


_INS = {
    "x": "x", "a_norm": "a_norm", "a_w_in": "a_w_in", "a_q_norm": "a_q_norm", "a_k_norm": "a_k_norm", "a_w_out": "a_w_out",
    "b_norm": "b_norm", "b_w_in": "b_w_in", "b_q_norm": "b_q_norm", "b_k_norm": "b_k_norm", "b_w_out": "b_w_out",
    "mem": "mem_2", "attn_norm_2": "attn_norm_2", "w_in": "w_in_2", "w_a2": "gla_w_a2_2", "b_a": "gla_b_a_2",
    "gla_norm": "gla_out_norm_2", "w_gla": "w_br_gla_2", "sb_q_norm": "sb_q_norm_2", "sb_k_norm": "sb_k_norm_2",
    "w_sb": "w_br_sb_2", "mem_norm_2": "mem_norm_2", "w_kv": "w_mem_kv_2", "mem_q_norm": "mem_q_norm_2",
    "mem_k_norm": "mem_k_norm_2", "w_mem": "w_br_mem_2", "w_o": "w_o_2", "ffn_norm_2": "ffn_norm_2",
    "w_gate_up": "w_gate_up_2", "w_down": "w_down_2",
}


def kernel(**inputs):
    import concourse.bacc as bacc
    from concourse.bass_utils import run_bass_kernel_spmd

    nc = bacc.Bacc("TRN2", target_bir_lowering=False, num_devices=1)
    arrays, io = {}, {}
    named = {name: np.ascontiguousarray(inputs[key]) for name, key in _INS.items()}
    named.update(constants())
    for name, a in named.items():
        arrays[f"in_{name}"] = a
        io[name] = nc.dram_tensor(f"in_{name}", a.shape, mybir.dt.from_np(a.dtype), kind="ExternalInput").ap()
    out = nc.dram_tensor("out_x", (1, T, D), F32, kind="ExternalOutput").ap()
    program(nc, io, out)
    r = run_bass_kernel_spmd(nc, [arrays], core_ids=[0])
    return r.results[0]["out_x"]
```

```python
from contextlib import ExitStack

import numpy as np
import concourse.bass as bass
from concourse import mybir

F32 = mybir.dt.float32
F32R = mybir.dt.float32r
I32 = mybir.dt.int32
ALU = mybir.AluOpType
ACT = mybir.ActivationFunctionType
AX = mybir.AxisListType

P = 128
T = 256
TT = T // P
D = 2048
KT = D // P
NB = 512
KC = 4
RAW = 2
SPL = 4
LEAD = 3
HD = 128
GROUPS = 4
HPG = 4
EPS = 1e-6
NEG = -1e30
TAKEN = -3e38
SCALE = float(HD) ** -0.5
N_KEEP = T // 4
IDX_HEADS, IDX_DIM = 16, 64
ATTENTION_HEADS = 2 * GROUPS * HPG
W0 = P + T
RSQRT_SEED = 1597463007.0

A_COLS = dict(q=0, k=2048, v=2560, gate=3072, qi=5120, ki=6144)
F_FF = 5632
FF_PARTS = ((0, 4), (4, 4), (8, 3))
GLA_HEADS, GLA_DK, GLA_DV, GLA_CHUNK, GLA_TAU = 4, 128, 256, 64, 16.0
SB_HEADS, MEM_HEADS, MEM_DH = 8, 4, 256
MIX_KC = 1024 // P // KC
IN_COLS = dict(gq=0, gk=512, gv=1024, gr=2048, ga=3072, sq=3088, sk=4112, sv=5136, mq=6160, gates=7184)
BIG = 3e38
NARROW = {0: 80, 37: 16}
B_COLS = dict(q=0, k=2048, v=2560, gate=3072)


class Count:

    def __init__(self, k=0):
        self.k, self.reg = k, None

    def __call__(self, d=0):
        v = self.k + d
        return v if self.reg is None else self.reg + v

    def step(self, n=1):
        self.k += n


def loop(eng, start, end, steps):
    with eng.Fori(start, end) as j:
        first = {c: c.k for c in steps}
        for c, per in steps.items():
            assert c.reg is None
            c.reg = (j - start) * per if start else j * per
        yield j
        for c, per in steps.items():
            assert c.k - first[c] == per, (c.k, first[c], per)
            c.reg, c.k = None, first[c] + per * (end - start)


def constants():
    def table(d):
        inv = (10000.0 ** (-np.arange(0, d, 2, dtype=np.float32) / np.float32(d))).astype(np.float32)
        ang = np.arange(T, dtype=np.float32)[:, None] * inv[None, :]
        c, s = np.cos(ang), np.sin(ang)
        both = np.stack([np.concatenate([c, c], 1), np.concatenate([-s, s], 1)])
        return both.reshape(2, TT, P, d).transpose(2, 0, 1, 3).astype(np.float32)

    i = np.arange(P)
    chunk = i // 64
    same = chunk[:, None] == chunk[None, :]
    causal = np.where(i[None, :] <= i[:, None], 0.0, NEG)
    mask = np.concatenate([causal, np.zeros((P, P)), causal], 1)
    squares = np.stack([
        np.eye(P),
        same & (i[:, None] <= i[None, :]),
        same & (i[:, None] > i[None, :]),
        i[:, None] > i[None, :],
        np.ones((P, P)),
        i[:, None] < i[None, :],
        np.where(i[:, None] <= i[None, :], BIG, 0.0),
        np.where(i[:, None] <= i[None, :], -BIG, 0.0),
    ]).astype(np.float32)
    ends = np.stack([chunk == 0, chunk == 1], 1).astype(np.float32)
    return {
        "c_rope128": table(HD), "c_rope64": table(IDX_DIM), "c_mask": mask.astype(np.float32),
        "c_squares": np.ascontiguousarray(squares.transpose(1, 0, 2)), "c_ends": ends,
    }


def program(nc, io, out):
    ctx = ExitStack()
    with ctx:
        base = (nc.sbuf_base + 63) // 64 * 64
        top = [base]

        def at(name, shape, offset, dt=F32):
            return nc.alloc_sbuf_tensor_at(name, shape, dt, offset=offset)

        def sb(name, shape, dt=F32):
            n = 4
            for s in shape[1:]:
                n *= s
            t = at(name, shape, top[0], dt)
            top[0] += (n + 31) // 32 * 32
            assert top[0] <= nc.sbuf_usable_end, (name, top[0])
            return t

        def sem(name):
            return ctx.enter_context(nc.semaphore(name))

        N_GAINS = 5 * KT + 6
        MEM_Q, MEM_K, SB_Q, SB_K = 5 * KT, 5 * KT + 2, 5 * KT + 4, 5 * KT + 5
        raw = sb("raw", [P, RAW, KC, NB])
        w_hi = sb("w_hi", [P, SPL, KC, NB], F32R)
        w_lo = sb("w_lo", [P, SPL, KC, NB], F32R)
        a_hi = [sb("a0_hi", [P, KT, T], F32R)]
        a_lo = [sb("a0_lo", [P, KT, T], F32R)]
        a1_at = top[0]
        a_hi.append(sb("a1_hi", [P, KT, T], F32R))
        a_lo.append(sb("a1_lo", [P, KT, T], F32R))
        base_x = top[0]
        x = sb("x", [P, TT, D])
        ident_t = sb("ident", [P, P])
        ident = ident_t[:]
        ends = sb("ends", [P, 2])
        gains = sb("gains", [P, N_GAINS])
        ss = sb("ss", [P, TT])
        ss_part = sb("ss_part", [P, 2, TT])
        rstd = sb("rstd", [P, TT])
        newton = sb("newton", [P, 4, 16])
        arena2 = top[0]
        rope = sb("rope", [P, 2, TT, HD])
        cmask = sb("cmask", [P, W0])
        qk_gain = sb("qk_gain", [P, 2, HD])
        rope_q = sb("rope_q", [P, 2, TT, HD])
        rope_k = sb("rope_k", [P, 2, TT, HD])
        arena = top[0]

        def area(name, shape, offset, dt=F32):
            n = 4
            for s in shape[1:]:
                n *= s
            assert arena + offset + n <= nc.sbuf_usable_end, (name, arena + offset + n, nc.sbuf_usable_end)
            return at(name, shape, arena + offset, dt)

        K = 1024
        kT = area("kT", [P, GROUPS, T], 0)
        v_nat = area("v_nat", [P, TT, GROUPS * HD], 4 * K)
        proj = area("proj", [P, TT, NB], 8 * K)
        rot = area("rot", [P, TT, NB], 12 * K)
        qT = area("qT", [P, HPG, T], 16 * K)
        rope_t = area("rope_t", [P, TT, NB], 16 * K)
        silu_g = area("silu_g", [P, TT, NB], 20 * K)
        o_gated = area("o_gated", [P, TT, NB], 24 * K)
        probs = area("probs", [P, 2, W0], 28 * K)
        probsT = area("probsT", [P, 2, W0], 31 * K)
        sel_mask = area("sel_mask", [P, W0], 34 * K)
        row = area("row", [P, 4, 2 * HPG], 35 * K + 512)
        qiT = at("qiT", [P, IDX_HEADS // 2, T], a1_at)
        kiT = at("kiT", [P, T], a1_at + 8 * K)
        ki2 = at("ki2", [P, TT, P], a1_at + 9 * K)
        rope64 = at("rope64", [P, 2, TT, IDX_DIM], a1_at + 10 * K)
        wi = at("wi", [P, TT, IDX_HEADS], a1_at + 11 * K)
        relus = at("relus", [P, 2, W0], a1_at + 12 * K)
        score_sum = at("score", [P, W0], a1_at + 15 * K)
        top8 = at("top8", [P, 8], a1_at + 17 * K)
        def area2(name, shape, offset, dt=F32):
            n = 4
            for s in shape[1:]:
                n *= s
            assert arena2 + offset + n <= nc.sbuf_usable_end, (name, arena2 + offset + n, nc.sbuf_usable_end)
            return at(name, shape, arena2 + offset, dt)

        a1_hi_end, a1_lo_end = a1_at + 8 * K, a1_at + 24 * K
        sq = area2("squares", [P, 7, P], 42 * K + 512)
        cum64, after64, after, ones, strict, at_most, at_least = (sq[:, n, :] for n in range(7))
        mem_nat = area2("mem_nat", [P, TT, D], 24 * K + 512)
        mkT = area2("mkT", [P, KT // 2, T], 0)
        mv = area2("mv", [P, TT, 1024], 8 * K)
        mqT = area2("mqT", [P, KT // 2, T], 16 * K)
        pre = area2("pre", [P, TT, NB], 24 * K)
        pre_t = area2("pre_t", [P, TT, NB], 28 * K)
        pre_t2 = area2("pre_t2", [P, TT, NB], 16 * K)
        m_probs = area2("m_probs", [P, 2, TT, T], 32 * K)
        m_probsT = area2("m_probsT", [P, 2, TT, T], 36 * K)
        stat = area2("stat", [P, 4, 8], 40 * K)
        mem_ss = area2("mem_ss", [P, TT], 41 * K)
        mem_rstd = area2("mem_rstd", [P, TT], 41 * K + 32)
        gq = area2("gq", [P, TT, NB], 24 * K)
        gk = area2("gk", [P, TT, NB], 28 * K)
        gv = at("gv", [P, TT, 1024], a1_hi_end)
        gr = at("gr", [P, TT, 1024], a1_lo_end)
        log_a = area2("log_a", [P, NB], 0)
        e_in = area2("e_in", [P, NB], 2 * K)
        e_neg = area2("e_neg", [P, NB], 4 * K)
        e_rest = area2("e_rest", [P, NB], 6 * K)
        kd = area2("kd", [P, NB], 8 * K)
        qeT = area2("qeT", [P, NB], 10 * K)
        keT = area2("keT", [P, NB], 12 * K)
        sT = area2("sT", [P, NB], 14 * K)
        state = area2("state", [P, GLA_HEADS, GLA_DV], 16 * K)
        g_out = area2("g_out", [P, GLA_HEADS, GLA_DV], 20 * K)
        g_sq = area2("g_sq", [P, GLA_HEADS, GLA_DV], 4 * K)
        w_a2 = area2("w_a2", [16, NB], 36 * K)
        b_a = area2("b_a", [P, NB], 38 * K)
        g_gain = area2("g_gain", [P, GLA_DV], 40 * K)
        gaT = area2("gaT", [16, T], 41 * K)
        ga = area2("ga", [P, TT, 16], 42 * K)
        decay = area2("decay", [P, TT, GLA_HEADS, 2], 42 * K + 128)
        sq_nat = at("sq_nat", [P, SB_HEADS, TT, HD], a1_hi_end)
        sk_nat = at("sk_nat", [P, SB_HEADS, TT, HD], a1_lo_end)
        sv_nat = area2("sv_nat", [P, TT, 1024], 0)
        sb_tmp = area2("sb_tmp", [P, TT, NB], 8 * K)
        qkT = area2("qkT", [P, 2, 2, T], 12 * K)
        soft_p = area2("soft_p", [P, 2, W0], 16 * K)
        neg_l = area2("neg_l", [P, 2, W0], 19 * K)
        stick = area2("stick", [P, 2, W0], 22 * K)
        sb_gain = area2("sb_gain", [P, 2], 25 * K)
        b_gate = area2("b_gate", [P, TT, NB], 32 * K)
        pre_q = at("pre_q", [P, TT, NB], base_x)
        note = [area2(f"note{i}", [P, 1], 42 * K + 256 + 32 * i) for i in range(4)]
        b_tmp = area2("b_tmp", [P, TT, NB], 28 * K)
        f_gate = area2("f_gate", [P, TT, NB], 0)
        f_mid = area2("f_mid", [P, TT, NB], 4 * K)
        x_mid = nc.dram_tensor("x_mid", (P, TT, D), F32, kind="Internal").ap()
        x_new = area("x_new", [P, 2, TT, NB], 0)
        row_sq2 = at("row_sq2", [P, TT, D], a1_at)
        sq_out = area("sq_out", [P, 2, TT, NB], 8 * K)
        row_sq = area("row_sq", [P, TT, D], 0)
        gain_rows = area("gain_rows", [N_GAINS, P], 20 * K)

        N_CONST, N_GAIN_LOADS = 6, 8

        def chunk_width(c, d):
            return NARROW.get((c.k + d) // KC, NB) if c.reg is None else NB

        SCORES_AT = (1, 3, 4, 5, 7)

        def score_heads(p):
            return range(2 * p, 2 * p + 2)

        def chunk_loads(c, d):
            n = 16 * ((c.k + d) // RAW + 1)
            return n if c.reg is None else c.reg * (16 // RAW) + n

        def halves(c, d, h):
            n = 2 * (c.k + d) + h
            return n if c.reg is None else c.reg * 2 + n

        def bank(name):
            return ctx.enter_context(nc.psum_tensor(name, [P, NB], F32))

        G = [[bank(f"gemm{b}_{t}") for t in range(TT)] for b in range(2)]
        M = [bank("turn0"), bank("turn1")]
        L = bank("logits")
        O = bank("mixed")

        raw_in = [[sem(f"raw_in{s}_{h}") for h in range(2)] for s in range(RAW)]
        hi_done = sem("hi_done")
        lo_done = sem("lo_done")
        chunk_done = sem("chunk_done")
        block_read = sem("block_read")
        m_full, m_hi, m_free = sem("m_full"), sem("m_hi"), sem("m_free")
        l_full, l_free = sem("l_full"), sem("l_free")
        o_full, o_free = sem("o_full"), sem("o_free")
        first_in = sem("first_in")
        gains_in = sem("gains_in")
        x_in = [sem(f"x_in{h}") for h in range(2)]
        const_in = sem("const_in")
        table_in = sem("table_in")
        mem_in, small_in = sem("mem_in"), sem("small_in")
        x_kept, x_back = sem("x_kept"), sem("x_back")
        a_seq, v_seq = sem("a_seq"), sem("v_seq")
        squares_ready = sem("squares_ready")
        relu_ready = sem("relu_ready")
        max_ready, probs_ready = sem("max_ready"), sem("probs_ready")
        gate_ready, silu_ready = sem("gate_ready"), sem("silu_ready")
        sig_ready = sem("sig_ready")
        xn_kept = sem("xn_kept")
        for_act, from_act = sem("for_act"), sem("from_act")
        rot_ready = sem("rot_ready")
        for_pe = sem("for_pe")
        gains_free = sem("gains_free")
        phase_done = sem("phase_done")
        x_final, out_done = sem("x_final"), sem("out_done")

        LAST_TWO = [(b, kc) for b in (2, 3) for kc in range(4)]
        ORDER_12 = [(0, 0), (0, 1), (0, 2), (1, 0), (1, 1), (1, 2), (0, 3), (1, 3)] + LAST_TWO
        ORDER_8 = [(0, 0), (0, 1), (1, 0), (1, 1), (0, 2), (1, 2), (0, 3), (1, 3)] + LAST_TWO
        SUM_AT, TURN_AT = (6, 7, 11, 15), (8, 9, 13)
        MERGED_GAPS = (7, 6, 11, 1)

        def chunks_of(w):
            return w.rearrange("(c k p) n -> p c k n", p=P, k=KC)

        wA, wAo, wB, wBo = (chunks_of(io[n][0]) for n in ("a_w_in", "a_w_out", "b_w_in", "b_w_out"))
        w_in, w_kv, w_o, w_gu, w_dn = (chunks_of(io[n][0]) for n in ("w_in", "w_kv", "w_o", "w_gate_up", "w_down"))
        w_branch = [chunks_of(io[n][0]) for n in ("w_gla", "w_sb", "w_mem")]
        w_gates = [w_in[:, :, :, IN_COLS["gates"] + n * D:IN_COLS["gates"] + (n + 1) * D] for n in range(3)]
        N_CHUNKS = 124 + 8 + 16 + 28 + 24 + 3 * 24 + 16 + 11 * 8 + 44

        block = ctx.enter_context(nc.Block())

        @block.sync
        def _(sp):
            c = Count()

            def load(view, kc, col, width=NB):
                s = c.k % RAW
                for h in range(2):
                    tiles = slice(h * KC // 2, (h + 1) * KC // 2)
                    if c.k >= RAW:
                        sp.wait_ge(lo_done, halves(c, -RAW, h + 1))
                    sp.dma_start(raw[:, s, tiles, 0:width],
                                 view[:, kc, tiles, bass.ds(col, width)]).then_inc(raw_in[s][h], 16)
                c.step()

            def load_block(view, col, width=NB):
                for kc in range(KT // KC):
                    load(view, kc, col, width)

            sp.dma_start(ident_t[:], io["c_squares"][:, 0, :]).then_inc(first_in, 16)
            for h in range(2):
                cols = slice(h * D // 2, (h + 1) * D // 2)
                for t in range(TT):
                    sp.dma_start(x[:, t, cols], io["x"][0, t * P:(t + 1) * P, cols]).then_inc(x_in[h], 16)
            load_block(wA, A_COLS["ki"], 80)
            for b in range(2):
                load_block(wA, A_COLS["qi"] + b * NB)
            for name in ("k", "v"):
                load_block(wA, A_COLS[name])
            for cols, w, w_out in ((A_COLS, wA, wAo), (B_COLS, wB, wBo)):
                if w is wB:
                    load_block(w, cols["k"])
                    load_block(w, cols["v"])
                for j in loop(sp, 0, GROUPS, {c: 8}):
                    load_block(w, cols["q"] + j * NB)
                    load_block(w, cols["gate"] + j * NB)
                for b, kc in ORDER_12:
                    load(w_out, kc, b * NB)
            for b in range(2):
                load_block(w_in, IN_COLS["mq"] + b * NB)
            for b in range(4):
                load_block(w_kv, b * NB)

            def load_branch(n):
                for j in loop(sp, 0, 2, {c: 12}):
                    for u in range(2):
                        col = j * (2 * NB) + u * NB
                        load_block(w_gates[n], col)
                        for kc in range(MIX_KC):
                            load(w_branch[n], kc, j * NB * 2 + u * NB)

            load_block(w_in, IN_COLS["ga"], 16)
            for b in range(6):
                load_block(w_in, IN_COLS["gq"] + b * NB)
            load_branch(2)
            for b in range(2):
                for name in ("sq", "sk", "sv"):
                    load_block(w_in, IN_COLS[name] + b * NB)
            load_branch(0)
            load_branch(1)
            for b, kc in ORDER_8:
                load(w_o, kc, b * NB)
            for b0, n in FF_PARTS:
                if n == 4:
                    for j in loop(sp, 0, n, {c: 8}):
                        load_block(w_gu, j * NB + b0 * NB)
                        load_block(w_gu, j * NB + (F_FF + b0 * NB))
                    for j in loop(sp, 0, 2, {c: 8}):
                        for u in range(2):
                            for kc in range(n):
                                load(w_dn, b0 + kc, j * (2 * NB) + u * NB)
                else:
                    for b in range(b0, b0 + n):
                        load_block(w_gu, b * NB)
                        load_block(w_gu, F_FF + b * NB)
                    for b in range(D // NB):
                        for kc in range(n):
                            load(w_dn, b0 + kc, b * NB)
            assert c.k == N_CHUNKS, (c.k, N_CHUNKS)
            out_t = out[0].rearrange("(t p) d -> p t d", p=P)
            for b in range(D // NB):
                sp.wait_ge(x_final, b + 1)
                sp.dma_start(out_t[:, :, b * NB:(b + 1) * NB], x[:, :, b * NB:(b + 1) * NB]).then_inc(out_done, 16)
            sp.wait_ge(out_done, 16 * (D // NB))

        @block.gpsimd
        def _(pool):
            n = 0
            for dst, src in (
                (ends[:], io["c_ends"]), (rope[:], io["c_rope128"]), (cmask[:], io["c_mask"]),
                (rope64[:], io["c_rope64"]),
                (qk_gain[:, 0, :], io["a_q_norm"][0].partition_broadcast(P)),
                (qk_gain[:, 1, :], io["a_k_norm"][0].partition_broadcast(P)),
            ):
                pool.dma_start(dst, src).then_inc(const_in, 16)
                n += 1
            assert n == N_CONST
            pool.wait_ge(gains_free, 1)
            pool.dma_start(qk_gain[:, 0, :], io["b_q_norm"][0].partition_broadcast(P)).then_inc(table_in, 16)
            pool.dma_start(qk_gain[:, 1, :], io["b_k_norm"][0].partition_broadcast(P)).then_inc(table_in, 16)
            pool.wait_ge(phase_done, 1)
            pool.dma_start(sq[:], io["c_squares"][:, 1:, :]).then_inc(small_in, 16)
            for t in range(TT):
                pool.dma_start(mem_nat[:, t, :], io["mem"][0, t * P:(t + 1) * P, :]).then_inc(mem_in, 16)
            for b in range(D // NB):
                pool.wait_ge(xn_kept, 5 + b)
                cols = slice(b * NB, (b + 1) * NB)
                pool.dma_start(x_mid[:, :, cols], x[:, :, cols]).then_inc(x_kept, 16)
            pool.wait_ge(phase_done, 2)
            pool.dma_start(w_a2[:], io["w_a2"][0]).then_inc(small_in, 16)
            pool.dma_start(b_a[:], io["b_a"][0].partition_broadcast(P)).then_inc(small_in, 16)
            pool.dma_start(g_gain[:], io["gla_norm"][0].partition_broadcast(P)).then_inc(small_in, 16)
            pool.wait_ge(phase_done, 3)
            pool.dma_start(x[:], x_mid).then_inc(x_back, 16)

        @block.scalar
        def _(act):
            c, m, mh = Count(), Count(), Count()
            nb, s_max, s_gate = Count(), Count(), Count()

            def split_hi(d=0):
                k = c.k + d
                n = chunk_width(c, d)
                if k >= SPL:
                    act.wait_ge(chunk_done, c(d + 1 - SPL))
                for h in range(2):
                    tiles = slice(h * KC // 2, (h + 1) * KC // 2)
                    act.wait_ge(raw_in[k % RAW][h], chunk_loads(c, d))
                    act.activation(w_hi[:, k % SPL, tiles, 0:n], raw[:, k % RAW, tiles, 0:n], ACT.Copy).then_inc(hi_done, 1)

            def ahead():
                if c.reg is not None or c.k + LEAD < N_CHUNKS:
                    split_hi(LEAD)
                c.step()

            def turned_hi(buf, k0, gain=None):
                act.wait_ge(m_full, m(1))
                src = M[m.k % 2][:].rearrange("p (k t) -> p k t", k=2)
                if gain is None:
                    last = act.activation(a_hi[buf][:, bass.ds(k0, 2), :], src, ACT.Copy)
                else:
                    for i in range(2):
                        last = act.activation(a_hi[buf][:, bass.ds(k0 + i, 1), :], src[:, i:i + 1, :], ACT.Copy,
                                              scale=gains[:, bass.ds(gain * KT + k0 + i, 1)])
                last.then_inc(m_hi, 1)
                m.step()
                mh.step()

            def exps():
                h = s_max.k
                act.wait_ge(max_ready, s_max(1))
                for t in range(TT):
                    cols = slice(t * P, t * P + P * (t + 1))
                    last = act.activation(probs[:, h % 2, cols], probs[:, h % 2, cols], ACT.Exp,
                                          bias=row[:, 1, 2 * (h % HPG) + t:2 * (h % HPG) + t + 1], scale=SCALE,
                                          accum_out=row[:, 2, 2 * (h % HPG) + t:2 * (h % HPG) + t + 1])
                last.then_inc(probs_ready, 1)
                s_max.step()

            def skip_turned(n=1):
                m.step(n)

            act.dma_start(gain_rows[0:16, :], io["a_norm"][0].rearrange("(k p) -> k p", p=P)).then_inc(first_in, 16)
            for dst, src in (
                (gain_rows[16:32, :], io["b_norm"][0].rearrange("(k p) -> k p", p=P)),
                (gain_rows[32:48, :], io["attn_norm_2"][0].rearrange("(k p) -> k p", p=P)),
                (gain_rows[48:64, :], io["mem_norm_2"][0].rearrange("(k p) -> k p", p=P)),
                (gain_rows[64:80, :], io["ffn_norm_2"][0].rearrange("(k p) -> k p", p=P)),
                (gain_rows[MEM_Q:MEM_Q + 2, :], io["mem_q_norm"][0].rearrange("(k p) -> k p", p=P)),
                (gain_rows[MEM_K:MEM_K + 2, :], io["mem_k_norm"][0].rearrange("(k p) -> k p", p=P)),
                (gain_rows[SB_Q:SB_Q + 1, :], io["sb_q_norm"]),
                (gain_rows[SB_K:SB_K + 1, :], io["sb_k_norm"]),
            ):
                act.dma_start(dst, src).then_inc(gains_in, 16)
            skip_turned()
            act.wait_ge(m_free, m())
            for h in range(KT // 2):
                turned_hi(0, 2 * h, 0)
                if h == 4:
                    split_hi(0)
            skip_turned()
            for d in range(1, LEAD):
                split_hi(d)
            for h in range(2):
                act.wait_ge(x_in[h], 16 * TT)
            for t in range(TT):
                last = act.activation(row_sq[:, t, :], x[:, t, :], ACT.Square, accum_out=ss[:, t:t + 1])
            last.then_inc(squares_ready, 1)

            def relu_heads(p):
                for h in score_heads(p):
                    act.wait_ge(m_full, m(1))
                    act.activation(relus[:, h % 2, :], M[m.k % 2][:, 0:W0], ACT.Relu).then_inc(relu_ready, 1)
                    m.step()

            for p in range(12):
                ahead()
            skip_turned(3)
            for p in range(8):
                ahead()
                if p == 2:
                    skip_turned(2)
                if p in SCORES_AT:
                    relu_heads(SCORES_AT.index(p))
            relu_heads(5)

            def gate():
                act.wait_ge(gate_ready, s_gate(1))
                act.activation(silu_g[:], silu_g[:], ACT.Silu).then_inc(silu_ready, 1)
                s_gate.step()

            def turn(with_heads, b0, scoring=False):
                for p in range(8):
                    ahead()
                    if with_heads and p < 4:
                        exps()
                    if with_heads and 1 <= p <= 4:
                        skip_turned()
                    if with_heads and p == 6:
                        turned_hi(1, b0)
                        turned_hi(1, b0 + 2)
                    if scoring and p == 1:
                        skip_turned(2)
                    if scoring and 2 <= p <= 3:
                        relu_heads(p + 4)
                    if p == 7:
                        skip_turned(2)
                        gate()
                        nb.step(2)

            def tail_heads(b0):
                for p in range(4):
                    exps()
                    if p:
                        skip_turned()
                    yield
                skip_turned()
                yield
                yield
                turned_hi(1, b0)
                turned_hi(1, b0 + 2)

            def keep_sum(b):
                act.wait_ge(block_read, nb(1))
                nb.step()
                act.activation(x[:, :, b * NB:(b + 1) * NB], x_new[:, b % 2], ACT.Copy)
                for t in range(TT):
                    last = act.activation(sq_out[:, b % 2, t, :], x_new[:, b % 2, t, :], ACT.Square,
                                          accum_out=ss_part[:, b % 2, t:t + 1])
                last.then_inc(xn_kept, 1)

            def turn_sum(b, gain):
                for i in range(2):
                    turned_hi(0, 4 * b + 2 * i, gain)

            def project_out(gain, steps):
                for p in range(16):
                    if p == 6:
                        for _ in steps:
                            pass
                    ahead()
                    next(steps, None)
                    for b in range(3):
                        if p == SUM_AT[b] + 1:
                            keep_sum(b)
                        if p == TURN_AT[b] + 1:
                            turn_sum(b, gain)

            def last_sum(gain):
                keep_sum(3)
                yield
                yield
                turn_sum(3, gain)
                yield

            nb.step(5)
            for layer in range(2):
                if layer:
                    steps = last_sum(layer)
                    for p in range(8):
                        ahead()
                        next(steps, None)
                    nb.step(2)
                    skip_turned(2)
                turn(False, 0, scoring=(layer == 0))
                for j in loop(act, 1, GROUPS, {c: 8, nb: 2, m: 8, mh: 2, s_max: 4, s_gate: 1}):
                    turn(True, j * 4 - 4)
                project_out(layer + 1, tail_heads(4 * GROUPS - 4))

            s_a, a_q = Count(), Count()

            def seq(ins):
                ins.then_inc(a_seq, 1)
                a_q.step()
                act.wait_ge(a_seq, a_q())

            def asked():
                act.wait_ge(for_act, s_a(1))
                s_a.step()

            def answered(ins):
                ins.then_inc(from_act, 1)

            def blocks(n, per=4, steps=iter(())):
                for _ in range(n):
                    for _ in range(per):
                        ahead()
                        next(steps, None)
                    nb.step()

            def log1p_exp(buf):
                asked()
                seq(act.activation(buf, buf, ACT.Exp))
                answered(act.activation(buf, buf, ACT.Ln, bias=1.0))

            def memory_steps():
                yield from last_sum(2)
                act.wait_ge(mem_in, 16 * TT)
                for t in range(TT):
                    last = act.activation(row_sq2[:, t, :], mem_nat[:, t, :], ACT.Square, accum_out=mem_ss[:, t:t + 1])
                answered(last)
                yield
                act.wait_ge(from_act, 1)
                for h in range(KT // 2):
                    turned_hi(1, 2 * h, 3)
                    if h % 2:
                        yield

            steps = memory_steps()
            for b in range(2):
                for _ in range(4):
                    ahead()
                    next(steps, None)
            for _ in steps:
                pass
            nb.step(2)
            skip_turned(2)
            blocks(1)
            skip_turned(2)
            blocks(1)
            skip_turned(2)
            blocks(1)
            skip_turned(2)
            blocks(1)
            def mem_steps():
                for h in range(MEM_HEADS):
                    yield
                    asked()
                    for t in range(TT):
                        last = act.activation(m_probs[:, h % 2, t, :], L[:, t * T:(t + 1) * T], ACT.Exp,
                                              bias=stat[:, 1, t:t + 1], scale=MEM_DH ** -0.5,
                                              accum_out=stat[:, 2, t:t + 1])
                    answered(last)
                    yield
                    yield
                    yield
                    skip_turned()
                    turned_hi(1, 2 * h)

            def gate_sigmoid():
                act.wait_ge(block_read, nb(1))
                act.activation(b_gate[:], b_gate[:], ACT.Sigmoid).then_inc(sig_ready, 1)

            def branch_beside(steps, to_end=True):
                for b in range(D // NB):
                    for p in range(6):
                        ahead()
                        next(steps, None)
                        if p == 3:
                            gate_sigmoid()
                    nb.step(2)
                if to_end:
                    for _ in steps:
                        pass

            def gla_steps():
                asked()
                answered(act.activation(gr[:], gr[:], ACT.Silu))
                yield
                skip_turned()
                for t in range(TT):
                    yield
                    log1p_exp(e_in[:])
                    yield
                    yield
                    act.wait_ge(l_full, ATTENTION_HEADS + MEM_HEADS + 3 * t + 2)
                    seq(act.activation(e_in[:], L[:], ACT.Exp, scale=1 / GLA_TAU))
                    seq(act.activation(e_neg[:], L[:], ACT.Exp, scale=-1 / GLA_TAU))
                    act.wait_ge(o_full, ATTENTION_HEADS + 2 * t + 1)
                    seq(act.activation(e_rest[:], O[:], ACT.Exp, scale=1 / GLA_TAU))
                    asked()
                    answered(act.activation(decay[:, t], decay[:, t], ACT.Exp, scale=1 / GLA_TAU))
                    skip_turned(1 + 2 + 1 + 4 - 2 * t)
                    for _ in range(8):
                        yield

            def gr_steps():
                for h in range(4):
                    yield
                    turned_hi(1, 2 * h)

            def sb_steps():
                def soft_part(pair, h):
                    act.wait_ge(l_full, ATTENTION_HEADS + MEM_HEADS + 3 * TT + 2 * pair + h + 1)
                    seq(act.activation(soft_p[:, h, :], L[:, 0:W0], ACT.Abs))
                    seq(act.activation(soft_p[:, h, :], soft_p[:, h, :], ACT.Exp, scale=-1.0))
                    answered(act.activation(soft_p[:, h, :], soft_p[:, h, :], ACT.Ln, bias=1.0))

                def weights(h):
                    asked()
                    answered(act.activation(stick[:, h, :], stick[:, h, :], ACT.Exp))

                for pair in range(SB_HEADS // 2):
                    yield
                    yield
                    soft_part(pair, 0)
                    yield
                    yield
                    soft_part(pair, 1)
                    weights(0)
                    yield
                    yield
                    weights(1)
                    yield
                    yield
                    skip_turned(2)
                    turned_hi(1, 8 + 2 * pair)

            steps = mem_steps()
            for b in range(7):
                blocks(1, steps=steps)
            for _ in steps:
                pass
            branch_beside(gla_steps())
            steps = gr_steps()

            def late_start():
                yield
                yield
                yield from sb_steps()

            for b in range(6):
                if b == 2:
                    steps = late_start()
                blocks(1, steps=steps)
            branch_beside(steps)

            def merged_steps():
                yield
                for b, gap in enumerate(MERGED_GAPS):
                    for _ in range(gap):
                        yield
                    turned_hi(1, 4 * b)
                    turned_hi(1, 4 * b + 2)

            steps = merged_steps()
            branch_beside(steps, False)
            project_out(4, steps)
            for b0, n in FF_PARTS:
                def ffn_turn(prev, b, steps=iter(())):
                    for p in range(8):
                        ahead()
                        next(steps, None)
                        if p == 2 and prev:
                            for i in range(2):
                                turned_hi(1, b * 4 - 4 + 2 * i)
                        if p == 3:
                            act.wait_ge(block_read, nb(1))
                            act.activation(f_gate[:], f_gate[:], ACT.Silu).then_inc(sig_ready, 1)
                    nb.step(2)

                ffn_turn(False, 0, last_sum(4) if b0 == 0 else iter(()))
                for j in loop(act, 1, n, {c: 8, nb: 2, m: 2, mh: 2}):
                    ffn_turn(True, j)
                for b in range(4):
                    for p in range(n):
                        ahead()
                        if b == 0 and p == 1:
                            for i in range(2):
                                turned_hi(1, n * 4 - 4 + 2 * i)
                    nb.step()

        @block.vector
        def _(v):
            c, nb, m, mh, l, o, q = Count(), Count(), Count(), Count(), Count(), Count(), Count()
            s_silu, s_relu, s_xn, s_rot = Count(), Count(), Count(), Count()

            def seq(ins):
                ins.then_inc(v_seq, 1)
                q.step()
                v.wait_ge(v_seq, q())

            def split_lo(d=0):
                k = c.k + d
                n = chunk_width(c, d)
                for h in range(2):
                    tiles = slice(h * KC // 2, (h + 1) * KC // 2)
                    v.wait_ge(hi_done, halves(c, d, h + 1))
                    v.tensor_tensor(w_lo[:, k % SPL, tiles, 0:n], raw[:, k % RAW, tiles, 0:n],
                                    w_hi[:, k % SPL, tiles, 0:n].bitcast(F32), ALU.subtract).then_inc(lo_done, 1)

            def ahead():
                if c.reg is not None or c.k + LEAD < N_CHUNKS:
                    split_lo(LEAD)
                c.step()

            def read_block(dst, width=NB, rows=rstd):
                v.wait_ge(chunk_done, c())
                for t in range(TT):
                    last = v.tensor_scalar(dst[:, t, 0:width], G[nb.k % 2][t][:, 0:width], rows[:, t:t + 1], None,
                                           ALU.mult)
                    if t == TT - 1:
                        last.then_inc(block_read, 1)
                    nb.step(t)
                v.wait_ge(block_read, nb())

            def turned_lo(buf, k0, gain=None):
                v.wait_ge(m_full, m(1))
                v.wait_ge(m_hi, mh(1))
                src = M[m.k % 2][:].rearrange("p (k t) -> p k t", k=2)
                if gain is None:
                    last = v.tensor_tensor(a_lo[buf][:, bass.ds(k0, 2), :], src,
                                           a_hi[buf][:, bass.ds(k0, 2), :].bitcast(F32), ALU.subtract)
                else:
                    for i in range(2):
                        last = v.scalar_tensor_tensor(
                            out=a_lo[buf][:, bass.ds(k0 + i, 1), :], in0=src[:, i:i + 1, :],
                            scalar=gains[:, bass.ds(gain * KT + k0 + i, 1)],
                            in1=a_hi[buf][:, bass.ds(k0 + i, 1), :].bitcast(F32), op0=ALU.mult, op1=ALU.subtract)
                last.then_inc(m_free, 1)
                m.step()
                mh.step()

            def turned_copy(dst):
                v.wait_ge(m_full, m(1))
                v.tensor_copy(dst, M[m.k % 2][:, 0:dst.free_size()]).then_inc(m_free, 1)
                m.step()

            def rsqrt(dst, src, width, n):
                a, y, z = (newton[:, i, 0:n] for i in range(3))
                yi = y.bitcast(I32)
                seq(v.tensor_scalar(a, src, 1.0 / width, EPS, ALU.mult, ALU.add))
                seq(v.tensor_scalar(yi, a.bitcast(I32), 1, None, ALU.arith_shift_right))
                seq(v.tensor_scalar(yi, yi, -1.0, RSQRT_SEED, ALU.mult, ALU.add))
                for step in range(3):
                    seq(v.tensor_tensor(z, y, y, ALU.mult))
                    seq(v.tensor_tensor(z, z, a, ALU.mult))
                    seq(v.tensor_scalar(z, z, -0.5, 1.5, ALU.mult, ALU.add))
                    seq(v.tensor_tensor(dst if step == 2 else y, y, z, ALU.mult))

            def heads_of(ap, hd):
                return ap.rearrange("p t (h d) -> p t h d", d=hd)

            def norm_heads(buf, hd, n, tmp=None, then=None):
                tmp = rope_t[:] if tmp is None else tmp
                seq(v.tensor_tensor(tmp, buf, buf, ALU.mult))
                ms = newton[:, 3, 0:n]
                ms3 = ms.rearrange("p (t h) -> p t h", t=TT)
                seq(v.tensor_reduce(ms3, heads_of(tmp, hd), AX.X, ALU.add))
                rsqrt(ms, ms, hd, n)
                by = ms3[:, :, :, None].to_broadcast([P, TT, n // TT, hd])
                last = v.tensor_tensor(heads_of(buf, hd), heads_of(buf, hd), by, ALU.mult)
                seq(last) if then is None else last.then_inc(then, 1)

            def rotate(dst, src, table, hd):
                n, h = src.shape[2] // hd, hd // 2
                s4, d4 = heads_of(src, hd), heads_of(dst, hd)
                t4 = heads_of(rope_t[:, :, 0:src.shape[2]], hd)
                cos, sin = (table[:, i, :, None, :].to_broadcast([P, TT, n, hd]) for i in range(2))
                v.tensor_tensor(t4, s4, cos, ALU.mult)
                v.tensor_tensor(d4[:, :, :, 0:h], s4[:, :, :, h:hd], sin[:, :, :, 0:h], ALU.mult)
                seq(v.tensor_tensor(d4[:, :, :, h:hd], s4[:, :, :, 0:h], sin[:, :, :, h:hd], ALU.mult))
                v.tensor_tensor(dst, dst, rope_t[:, :, 0:src.shape[2]], ALU.add).then_inc(rot_ready, 1)
                s_rot.step()

            def gain_tables():
                for i, dst in ((0, rope_q), (1, rope_k)):
                    g = qk_gain[:, i, None, :].to_broadcast([P, TT, HD])
                    v.tensor_tensor(dst[:, 0], rope[:, 0], g, ALU.mult)
                    h = HD // 2
                    v.tensor_tensor(dst[:, 1, :, 0:h], rope[:, 1, :, 0:h], g[:, :, h:HD], ALU.mult)
                    last = v.tensor_tensor(dst[:, 1, :, h:HD], rope[:, 1, :, h:HD], g[:, :, 0:h], ALU.mult)
                seq(last)

            def soft(r):
                h = r % 2
                v.wait_ge(l_full, l(1))
                v.memset(row[:, 3, 2 * r:2 * r + 2], 0.0)
                mx, nm = row[:, 0, 2 * r:2 * r + 2], row[:, 1, 2 * r:2 * r + 2]
                for t in range(TT):
                    cols = slice(t * P, t * P + P * (t + 1))
                    last = v.tensor_tensor_reduce(out=probs[:, h, cols], in0=L[:, cols], in1=mask_of()[:, cols], scale=1.0,
                                                  scalar=TAKEN, op0=ALU.add, op1=ALU.max, accum_out=mx[:, t:t + 1])
                last.then_inc(l_free, 1)
                l.step()
                v.wait_ge(l_free, l())
                v.tensor_scalar(nm, mx, -SCALE, None, ALU.mult).then_inc(max_ready, 1)

            def weigh(r):
                v.wait_ge(o_full, o(1))
                seq(v.reciprocal(row[:, 3, 2 * r:2 * r + 2], row[:, 2, 2 * r:2 * r + 2]))
                if r == 0:
                    v.wait_ge(silu_ready, s_silu(1))
                    s_silu.step()
                for t in range(TT):
                    last = v.scalar_tensor_tensor(
                        out=o_gated[:, t, r * HD:(r + 1) * HD], in0=O[:, (r % 2) * T + t * P:(r % 2) * T + (t + 1) * P],
                        scalar=row[:, 3, 2 * r + t:2 * r + t + 1], in1=silu_g[:, t, r * HD:(r + 1) * HD],
                        op0=ALU.mult, op1=ALU.mult)
                last.then_inc(o_free, 1)
                o.step()

            def score(p):
                for h in score_heads(p):
                    v.wait_ge(relu_ready, s_relu(1))
                    s_relu.step()
                    prev = cmask if h == 0 else score_sum
                    for t in range(TT):
                        cols = slice(t * P, t * P + P * (t + 1))
                        last = v.scalar_tensor_tensor(out=score_sum[:, cols], in0=relus[:, h % 2, cols],
                                                      scalar=wi[:, t, h:h + 1], in1=prev[:, cols],
                                                      op0=ALU.mult, op1=ALU.add)
                    last.then_inc(m_free, 1)
                    m.step()
                    v.wait_ge(m_free, m())

            def keep_largest(t):
                cols = slice(t * P, t * P + P * (t + 1))
                for _ in range(N_KEEP // 8):
                    seq(v.max(top8[:], score_sum[:, cols]))
                    seq(v.match_replace(score_sum[:, cols], top8[:], score_sum[:, cols], TAKEN))
                seq(v.tensor_scalar(score_sum[:, cols], score_sum[:, cols], TAKEN / 2, NEG, ALU.is_gt, ALU.mult))
                seq(v.tensor_tensor(sel_mask[:, cols], score_sum[:, cols], cmask[:, cols], ALU.add))

            masks = [cmask]

            def mask_of():
                return masks[0]

            def turn(with_heads, b0, scoring=False):
                for p in range(8):
                    if p == 4:
                        read_query()
                    ahead()
                    if scoring and p == 1:
                        keys_turned()
                    if scoring and 2 <= p <= 3:
                        score(p + 4)
                    if scoring and p == 3:
                        keep_largest(0)
                        keep_largest(1)
                    if with_heads:
                        if p < 4:
                            soft(p)
                        if 1 <= p <= 4:
                            turned_copy(probsT[:, (p - 1) % 2, :])
                        if 2 <= p <= 5:
                            weigh(p - 2)
                    if p == 5:
                        rotate(rot[:], proj[:], rope_q, HD)
                    if p == 4:
                        norm_heads(proj[:], HD, TT * HPG)
                    if with_heads and p == 6:
                        turned_lo(1, b0)
                        turned_lo(1, b0 + 2)
                    if p == 7:
                        for i in range(2):
                            turned_copy(qT[:, 2 * i:2 * i + 2, :].rearrange("p h t -> p (h t)"))
                        read_gate()

            def read_query():
                v.wait_ge(chunk_done, c())
                for t in range(TT):
                    last = v.tensor_scalar(proj[:, t, :], G[nb.k % 2][t][:], rstd[:, t:t + 1], None, ALU.mult)
                last.then_inc(block_read, 1)
                nb.step()
                v.wait_ge(block_read, nb())

            def read_gate():
                v.wait_ge(chunk_done, c())
                for t in range(TT):
                    last = v.tensor_scalar(silu_g[:, t, :], G[nb.k % 2][t][:], rstd[:, t:t + 1], None, ALU.mult)
                last.then_inc(block_read, 1)
                nb.step()
                v.wait_ge(block_read, nb())
                v.tensor_scalar(ss_part[:, 0, 0:1], ss_part[:, 0, 0:1], 1.0, None, ALU.mult).then_inc(gate_ready, 1)

            def tail_heads(b0):
                for p in range(6):
                    if p < 4:
                        soft(p)
                    if 1 <= p <= 4:
                        turned_copy(probsT[:, (p - 1) % 2, :])
                    if 2 <= p:
                        weigh(p - 2)
                    yield
                turned_lo(1, b0)
                turned_lo(1, b0 + 2)

            def turn_sum(b, gain):
                v.wait_ge(xn_kept, s_xn(1))
                s_xn.step()
                seq(v.tensor_tensor(ss[:], ss[:], ss_part[:, b % 2, :], ALU.add))
                for i in range(2):
                    turned_lo(0, 4 * b + 2 * i, gain)

            def project_out(gain, steps, then=None, back=False):
                for p in range(16):
                    if p == 6:
                        for _ in steps:
                            pass
                        seq(v.memset(ss[:], 0.0))
                    ahead()
                    next(steps, None)
                    if p in SUM_AT:
                        b = SUM_AT.index(p)
                        if back and b == 0:
                            v.wait_ge(x_back, 16)
                        v.wait_ge(chunk_done, c())
                        for t in range(TT):
                            last = v.tensor_tensor(x_new[:, b % 2, t, :], G[nb.k % 2][t][:],
                                                   x[:, t, b * NB:(b + 1) * NB], ALU.add)
                        last.then_inc(block_read, 1)
                        nb.step()
                    if then is not None and p == SUM_AT[1]:
                        then()
                    for b in range(3):
                        if p == TURN_AT[b] + 1:
                            turn_sum(b, gain)

            def last_sum(gain):
                yield
                yield
                turn_sum(3, gain)
                rsqrt(rstd[:], ss[:], D, TT)
                yield

            v.memset(ss_part[:], 0.0)
            turned_copy(gains[:, 0:KT])
            for h in range(KT // 2):
                turned_lo(0, 2 * h, 0)
                if h == 4:
                    split_lo(0)
            v.wait_ge(m_full, m(1))
            v.tensor_copy(gains[:, KT:N_GAINS], M[m.k % 2][:, KT:N_GAINS]).then_inc(m_free, 1)
            m.step()
            for d in range(1, LEAD):
                split_lo(d)
            v.wait_ge(const_in, 16 * N_CONST)
            gain_tables()
            v.tensor_copy(newton[:, 3, 15:16], rope[:, 0, 0, 0:1]).then_inc(gains_free, 1)
            v.wait_ge(squares_ready, 1)
            rsqrt(rstd[:], ss[:], D, TT)

            for _ in range(4):
                ahead()
            read_block(proj, width=80)
            v.tensor_scalar(wi[:], proj[:, :, IDX_DIM:80], IDX_HEADS ** -0.5 * IDX_DIM ** -0.5, None, ALU.mult)
            rotate(ki2[:, :, 0:IDX_DIM], proj[:, :, 0:IDX_DIM], rope64, IDX_DIM)
            v.wait_ge(rot_ready, s_rot())
            v.tensor_copy(ki2[:, :, IDX_DIM:P], ki2[:, :, 0:IDX_DIM]).then_inc(rot_ready, 1)
            s_rot.step()
            for b in range(2):
                for p in range(4):
                    ahead()
                    if p == 2 and b == 0:
                        turned_copy(kiT[:])
                    if p == 2 and b == 1:
                        for i in range(2):
                            turned_copy(qiT[:, 2 * i:2 * i + 2, :].rearrange("p h t -> p (h t)"))
                read_block(proj)
                rotate(rot[:], proj[:], rope64, IDX_DIM)

            def keys_turned():
                for i in range(2):
                    turned_copy(kT[:, 2 * i:2 * i + 2, :].rearrange("p h t -> p (h t)"))

            def index_keys_and_values():
                for p in range(8):
                    ahead()
                    if p == 2:
                        for i in range(2):
                            turned_copy(qiT[:, 4 + 2 * i:6 + 2 * i, :].rearrange("p h t -> p (h t)"))
                    if p in SCORES_AT:
                        score(SCORES_AT.index(p))
                    if p == 3:
                        read_block(proj)
                    if p == 4:
                        norm_heads(proj[:], HD, TT * HPG)
                    if p == 5:
                        rotate(rot[:], proj[:], rope_k, HD)
                score(5)
                read_block(v_nat)

            def keys_and_values(steps):
                for _ in range(4):
                    ahead()
                    next(steps, None)
                read_block(proj)
                norm_heads(proj[:], HD, TT * HPG)
                rotate(rot[:], proj[:], rope_k, HD)
                for _ in range(4):
                    ahead()
                    next(steps, None)
                for _ in steps:
                    pass
                read_block(v_nat)
                keys_turned()

            def buffers_free():
                v.tensor_copy(newton[:, 3, 14:15], ident[:, 0:1]).then_inc(phase_done, 1)

            for layer in range(2):
                masks[0] = (sel_mask, cmask)[layer]
                if layer:
                    v.wait_ge(table_in, 32)
                    gain_tables()
                    keys_and_values(last_sum(layer))
                else:
                    index_keys_and_values()
                turn(False, 0, scoring=(layer == 0))
                for j in loop(v, 1, GROUPS, {c: 8, nb: 2, m: 8, mh: 2, l: 4, o: 4, s_silu: 1, s_rot: 1, q: 23}):
                    turn(True, j * 4 - 4)
                project_out(layer + 1, tail_heads(4 * GROUPS - 4), buffers_free if layer else None)

            s_a, s_sig = Count(), Count()

            def ask(ins):
                ins.then_inc(for_act, 1)

            def answer():
                s_a.step()
                v.wait_ge(from_act, s_a())

            def block_of(dst, width=NB, rows=rstd, steps=iter(())):
                for _ in range(4):
                    ahead()
                    next(steps, None)
                read_block(dst, width, rows)

            def turned_scaled(dst, cols):
                v.wait_ge(m_full, m(1))
                src = M[m.k % 2][:].rearrange("p (k t) -> p k t", k=2)
                for i in range(2):
                    last = v.tensor_scalar(dst[:, i, :], src[:, i, :], cols[i], None, ALU.mult)
                last.then_inc(m_free, 1)
                m.step()

            def gain_cols(first):
                return [gains[:, first + i:first + i + 1] for i in range(2)]

            def memory_steps():
                yield from last_sum(2)
                yield
                for h in range(KT // 2):
                    turned_lo(1, 2 * h, 3)
                    if h == 3:
                        norm_heads(pre_q[:], MEM_DH, 2 * TT, pre_t2[:], for_pe)
                    if h % 2:
                        yield

            steps = memory_steps()
            for _ in range(4):
                ahead()
                next(steps, None)
            v.wait_ge(x_kept, 16 * (D // NB))
            read_block(pre_q[:])
            for _ in range(4):
                ahead()
                next(steps, None)
            for _ in steps:
                pass
            answer()
            rsqrt(mem_rstd[:], mem_ss[:], D, TT)
            read_block(pre[:])
            norm_heads(pre[:], MEM_DH, 2 * TT, pre_t[:], for_pe)

            def take_turned(dst, h0, gain):
                for i in range(2):
                    turned_scaled(dst[:, h0 + 2 * i:h0 + 2 * i + 2, :], gain_cols(gain))

            for p in range(4):
                ahead()
                if p == 1:
                    take_turned(mqT, 0, MEM_Q)
            take_turned(mqT, 4, MEM_Q)
            read_block(pre_q[:], rows=mem_rstd)
            norm_heads(pre_q[:], MEM_DH, 2 * TT, pre_t[:], for_pe)
            for p in range(4):
                ahead()
                if p == 3:
                    take_turned(mkT, 0, MEM_K)
            read_block(pre[:], rows=mem_rstd)
            norm_heads(pre[:], MEM_DH, 2 * TT, pre_t[:], for_pe)
            for p in range(4):
                ahead()
                if p == 3:
                    take_turned(mkT, 4, MEM_K)
            read_block(mv[:, :, 0:NB], rows=mem_rstd)
            block_of(mv[:, :, NB:2 * NB], rows=mem_rstd)
            def mem_steps():
                for h in range(MEM_HEADS):
                    yield
                    v.wait_ge(l_full, l(1))
                    l.step()
                    seq(v.tensor_reduce(stat[:, 0, 0:2], L[:].rearrange("p (t m) -> p t m", t=TT), AX.X, ALU.max))
                    ask(v.tensor_scalar(stat[:, 1, 0:2], stat[:, 0, 0:2], -MEM_DH ** -0.5, None, ALU.mult))
                    answer()
                    seq(v.reciprocal(stat[:, 3, 0:2], stat[:, 2, 0:2]))
                    for t in range(TT):
                        last = v.tensor_scalar(m_probs[:, h % 2, t, :], m_probs[:, h % 2, t, :], stat[:, 3, t:t + 1],
                                               None, ALU.mult)
                    last.then_inc(l_free, 1)
                    yield
                    yield
                    turned_copy(m_probsT[:, h % 2].rearrange("p s t -> p (s t)"))
                    yield
                    turned_lo(1, 2 * h)
                v.tensor_copy(stat[:, 0, 4:5], stat[:, 0, 0:1]).then_inc(phase_done, 1)

            def read_gates():
                v.wait_ge(chunk_done, c())
                for t in range(TT):
                    last = v.tensor_scalar(b_gate[:, t, :], G[nb.k % 2][t][:], rstd[:, t:t + 1], None, ALU.mult)
                last.then_inc(block_read, 1)
                nb.step()

            def merge(at_col, first, final=False):
                v.wait_ge(sig_ready, s_sig(1))
                s_sig.step()
                v.wait_ge(chunk_done, c())
                for t in range(TT):
                    dst = x[:, t, at_col] if first else b_tmp[:, t, :]
                    last = v.tensor_tensor(dst, G[nb.k % 2][t][:], b_gate[:, t, :], ALU.mult)
                last.then_inc(block_read, 1)
                nb.step()
                if not first:
                    v.wait_ge(block_read, nb())
                    last = v.tensor_tensor(x[:, :, at_col], x[:, :, at_col], b_tmp[:], ALU.add)
                    last.then_inc(for_pe, 1) if final else seq(last)

            def branch_beside(steps, first, final=False):
                for b in range(D // NB):
                    for p in range(6):
                        ahead()
                        next(steps, None)
                        if p == 3:
                            read_gates()
                    merge(slice(b * NB, (b + 1) * NB), first, final)
                if not final:
                    for _ in steps:
                        pass

            def gla_steps():
                ask(v.tensor_copy(note[0][:], ga[:, 0, 0:1]))
                yield
                v.wait_ge(m_full, m(1))
                v.tensor_copy(gaT[:], M[m.k % 2][0:16, 0:T]).then_inc(m_free, 1)
                m.step()
                v.wait_ge(small_in, 64)
                for t in range(TT):
                    yield
                    v.wait_ge(l_full, l(1))
                    l.step()
                    v.tensor_tensor(log_a[:], L[:], b_a[:], ALU.add).then_inc(l_free, 1)
                    v.wait_ge(l_free, l())
                    if t == 0:
                        answer()
                    ask(v.scalar_tensor_tensor(out=e_in[:], in0=log_a[:], scalar=-1.0, in1=log_a[:], op0=ALU.mult, op1=ALU.min))
                    answer()
                    v.scalar_tensor_tensor(out=log_a[:], in0=log_a[:], scalar=0.0, in1=e_in[:], op0=ALU.min,
                                           op1=ALU.subtract).then_inc(for_pe, 1)
                    yield
                    yield
                    v.wait_ge(m_full, m(1))
                    ask(v.tensor_copy(decay[:, t].rearrange("p h e -> p (h e)"), M[m.k % 2][:, 0:2 * GLA_HEADS]))
                    answer()
                    v.tensor_scalar(note[1][:], note[0][:], 1.0, None, ALU.mult).then_inc(m_free, 1)
                    m.step()
                    v.wait_ge(l_full, l(1))
                    v.wait_ge(o_full, o(1))
                    v.scalar_tensor_tensor(out=gq[:, t, :], in0=gq[:, t, :], scalar=GLA_DK ** -0.5, in1=e_in[:],
                                           op0=ALU.mult, op1=ALU.mult).then_inc(l_free, 1)
                    l.step()
                    v.tensor_tensor(kd[:], gk[:, t, :], e_rest[:], ALU.mult).then_inc(o_free, 1)
                    o.step()
                    v.tensor_tensor(gk[:, t, :], gk[:, t, :], e_neg[:], ALU.mult).then_inc(for_pe, 1)
                    yield
                    yield
                    turned_copy(qeT[:])
                    turned_copy(keT[:])
                    yield
                    v.wait_ge(m_full, m(1))
                    s4 = sT[:].rearrange("p (h t) -> p h t", h=GLA_HEADS)
                    bound = [b[:, None, :].to_broadcast([P, GLA_HEADS, P]) for b in (at_most, at_least)]
                    v.tensor_tensor(s4, M[m.k % 2][:].rearrange("p (h t) -> p h t", h=GLA_HEADS), bound[0],
                                    ALU.min).then_inc(m_free, 1)
                    m.step()
                    v.wait_ge(m_free, m())
                    v.tensor_tensor(s4, s4, bound[1], ALU.max).then_inc(for_pe, 1)
                    for half in range(2):
                        yield
                        n = 2 * t + half
                        if n == 3:
                            continue
                        for pair in range(2):
                            v.wait_ge(m_full, m(1))
                            for i in range(2):
                                h, src = 2 * pair + i, M[m.k % 2][:, i * GLA_DV:(i + 1) * GLA_DV]
                                if n == 0:
                                    last = v.tensor_copy(state[:, h, :], src)
                                else:
                                    last = v.scalar_tensor_tensor(out=state[:, h, :], in0=state[:, h, :],
                                                                  scalar=decay[:, t, h, half:half + 1], in1=src,
                                                                  op0=ALU.mult, op1=ALU.add)
                            last.then_inc(m_free, 1)
                            m.step()
                            v.wait_ge(m_free, m())
                    v.wait_ge(l_full, l(1))
                    v.wait_ge(o_full, o(1))
                    v.tensor_copy(g_out[:, 0:2, :].rearrange("p h d -> p (h d)"), L[:]).then_inc(l_free, 1)
                    v.tensor_copy(g_out[:, 2:4, :].rearrange("p h d -> p (h d)"), O[:]).then_inc(o_free, 1)
                    l.step()
                    o.step()
                    v.wait_ge(l_free, l())
                    v.wait_ge(o_free, o())
                    yield
                    seq(v.tensor_tensor(g_sq[:], g_out[:], g_out[:], ALU.mult))
                    ms = newton[:, 3, 0:GLA_HEADS]
                    seq(v.tensor_reduce(ms, g_sq[:], AX.X, ALU.add))
                    rsqrt(ms, ms, GLA_DV, GLA_HEADS)
                    seq(v.tensor_tensor(g_out[:], g_out[:], ms[:, :, None].to_broadcast([P, GLA_HEADS, GLA_DV]), ALU.mult))
                    seq(v.tensor_tensor(g_out[:], g_out[:], g_gain[:, None, :].to_broadcast([P, GLA_HEADS, GLA_DV]), ALU.mult))
                    gr4 = gr[:, t, :].rearrange("p (h d) -> p h d", h=GLA_HEADS)
                    v.tensor_tensor(gr4, gr4, g_out[:], ALU.mult).then_inc(for_pe, 1)
                    yield
                    yield

            def gr_steps():
                for h in range(4):
                    yield
                    turned_lo(1, 2 * h)

            def sb_steps():
                def keep(h):
                    v.wait_ge(l_full, l(1))
                    l.step()
                    answer()
                    v.scalar_tensor_tensor(out=stick[:, h, :], in0=L[:, 0:W0], scalar=0.0, in1=soft_p[:, h, :],
                                           op0=ALU.min, op1=ALU.subtract)
                    v.scalar_tensor_tensor(out=neg_l[:, h, :], in0=L[:, 0:W0], scalar=0.0, in1=soft_p[:, h, :],
                                           op0=ALU.max, op1=ALU.add).then_inc(l_free, 1)
                    v.wait_ge(l_free, l())
                    diag = neg_l[:, h, :].rearrange("p (b t) -> p b t", b=3)[:, 0:3:2, :]
                    v.tensor_tensor(diag, diag, strict[:, None, :].to_broadcast([P, 2, P]), ALU.mult).then_inc(for_pe, 1)

                def weights(h):
                    v.wait_ge(o_full, o(1))
                    o.step()
                    v.tensor_tensor(stick[:, h, :], stick[:, h, :], O[:, 0:W0], ALU.subtract).then_inc(o_free, 1)
                    v.wait_ge(o_free, o())
                    ask(v.tensor_copy(note[2][:], ident[:, 0:1]))
                    answer()
                    diag = stick[:, h, :].rearrange("p (b t) -> p b t", b=3)[:, 0:3:2, :]
                    v.tensor_tensor(diag, diag, strict[:, None, :].to_broadcast([P, 2, P]), ALU.mult).then_inc(for_pe, 1)

                for pair in range(SB_HEADS // 2):
                    yield
                    turned_scaled(qkT[:, 0], [sb_gain[:, 0:1], sb_gain[:, 1:2]])
                    yield
                    turned_scaled(qkT[:, 1], [sb_gain[:, 0:1], sb_gain[:, 1:2]])
                    keep(0)
                    yield
                    yield
                    keep(1)
                    weights(0)
                    yield
                    yield
                    weights(1)
                    yield
                    yield
                    turned_lo(1, 8 + 2 * pair)

            def sb_block(dst, steps):
                for _ in range(4):
                    ahead()
                    next(steps, None)
                v.wait_ge(chunk_done, c())
                for t in range(TT):
                    last = v.tensor_scalar(dst[:, :, t, :], G[nb.k % 2][t][:].rearrange("p (h d) -> p h d", d=HD),
                                           rstd[:, t:t + 1], None, ALU.mult)
                last.then_inc(block_read, 1)
                nb.step()
                v.wait_ge(block_read, nb())

            def norm_sb(buf):
                tmp = sb_tmp[:].rearrange("p t (h d) -> p (t h) d", d=HD)
                b3 = buf.rearrange("p h t d -> p (h t) d")
                seq(v.tensor_tensor(tmp, b3, b3, ALU.mult))
                ms = newton[:, 3, 0:TT * 4]
                seq(v.tensor_reduce(ms, tmp, AX.X, ALU.add))
                rsqrt(ms, ms, HD, TT * 4)
                seq(v.tensor_tensor(b3, b3, ms[:, :, None].to_broadcast([P, TT * 4, HD]), ALU.mult))

            steps = mem_steps()
            block_of(ga[:], width=16, steps=steps)
            block_of(gq[:], steps=steps)
            block_of(gk[:], steps=steps)
            for dst in (gv, gr):
                for b in range(2):
                    block_of(dst[:, :, b * NB:(b + 1) * NB], steps=steps)
            for _ in steps:
                pass
            branch_beside(gla_steps(), True)
            v.tensor_scalar(sb_gain[:, 0:1], gains[:, SB_Q:SB_Q + 1], HD ** -0.5, None, ALU.mult)
            seq(v.tensor_copy(sb_gain[:, 1:2], gains[:, SB_K:SB_K + 1]))
            steps = gr_steps()
            for b in range(2):
                for nat in (sq_nat, sk_nat):
                    sb_block(nat[:, 4 * b:4 * b + 4], steps)
                    norm_sb(nat[:, 4 * b:4 * b + 4])
                if b == 0:
                    v.tensor_copy(note[2][:], ident[:, 0:1]).then_inc(for_pe, 1)
                    steps = sb_steps()
                    for p in range(4):
                        ahead()
                        if p >= 2:
                            next(steps, None)
                    read_block(sv_nat[:, :, 0:NB])
                else:
                    block_of(sv_nat[:, :, NB:2 * NB], steps=steps)
            branch_beside(steps, False)

            def merged_steps():
                yield
                for b, gap in enumerate(MERGED_GAPS):
                    for _ in range(gap):
                        yield
                    turned_lo(1, 4 * b)
                    turned_lo(1, 4 * b + 2)
                v.wait_ge(m_free, m())
                v.tensor_copy(note[3][:], ident[:, 0:1]).then_inc(phase_done, 1)

            steps = merged_steps()
            branch_beside(steps, False, True)
            project_out(4, steps, back=True)
            for b0, n in FF_PARTS:
                def ffn_turn(prev, b, steps=iter(())):
                    for p in range(8):
                        ahead()
                        next(steps, None)
                        if p == 2 and prev:
                            for i in range(2):
                                turned_lo(1, b * 4 - 4 + 2 * i)
                        if p == 3:
                            v.wait_ge(chunk_done, c())
                            for t in range(TT):
                                last = v.tensor_scalar(f_gate[:, t, :], G[nb.k % 2][t][:], rstd[:, t:t + 1], None, ALU.mult)
                            last.then_inc(block_read, 1)
                            nb.step()
                        if p == 7:
                            v.wait_ge(chunk_done, c())
                            v.wait_ge(sig_ready, s_sig(1))
                            s_sig.step()
                            for t in range(TT):
                                last = v.scalar_tensor_tensor(out=f_mid[:, t, :], in0=G[nb.k % 2][t][:],
                                                              scalar=rstd[:, t:t + 1], in1=f_gate[:, t, :],
                                                              op0=ALU.mult, op1=ALU.mult)
                            last.then_inc(block_read, 1)
                            nb.step()

                def add_down(b, chunks, done=block_read):
                    for p in range(chunks):
                        ahead()
                        if b == 0 and p == 1:
                            for i in range(2):
                                turned_lo(1, n * 4 - 4 + 2 * i)
                    v.wait_ge(chunk_done, c())
                    for t in range(TT):
                        dst = x[:, t, bass.ds(b * NB, NB)]
                        last = v.tensor_tensor(dst, G[nb.k % 2][t][:], dst, ALU.add)
                    last.then_inc(done, 1)
                    nb.step()

                ffn_turn(False, 0, last_sum(4) if b0 == 0 else iter(()))
                for j in loop(v, 1, n, {c: 8, nb: 2, m: 2, mh: 2, s_sig: 1}):
                    ffn_turn(True, j)
                for b in range(4):
                    if n == 4:
                        add_down(b, n)
                    else:
                        add_down(b, n, block_read if b < 2 else x_final)
                        if b < 2:
                            v.wait_ge(block_read, nb())
                            v.tensor_copy(note[3][:], ident[:, 0:1]).then_inc(x_final, 1)

        @block.tensor
        def _(pe):
            c, nb, m, l, o = Count(), Count(), Count(), Count(), Count()
            s_rot, s_probs = Count(), Count()

            def chunk(buf, kc, n_kc, bank2, width=NB, k0=0):
                s = c.k % SPL
                pe.wait_ge(lo_done, halves(c, 0, 2))
                for t in range(TT):
                    toks = slice(t * P, (t + 1) * P)
                    for i in range(KC):
                        k = kc * KC + i
                        dst = bank2[t][:, 0:width]
                        xh, xl = a_hi[buf][:, k0 + k, toks], a_lo[buf][:, k0 + k, toks]
                        wh, wl = w_hi[:, s, i, 0:width], w_lo[:, s, i, 0:width]
                        pe.matmul(dst, xh, wh, start=(k == 0), stop=False)
                        pe.matmul(dst, xh, wl, start=False, stop=False)
                        last = pe.matmul(dst, xl, wh, start=False, stop=(k == n_kc * KC - 1))
                last.then_inc(chunk_done, 1)
                c.step()

            def bank_for_block():
                if nb.k >= 2:
                    pe.wait_ge(block_read, nb(-1))
                nb.step()
                return G[(nb.k - 1) % 2]

            def gemm(buf, n_kc=KT // KC, width=NB, k0=0, steps=iter(())):
                dst = bank_for_block()
                for kc in range(n_kc):
                    chunk(buf, kc, n_kc, dst, width, k0)
                    next(steps, None)

            def turned_bank():
                if m.k >= 2:
                    pe.wait_ge(m_free, m(-1))
                m.step()
                return M[(m.k - 1) % 2]

            def turn_two(src, f0):
                dst = turned_bank()
                for i in range(2):
                    for t in range(TT):
                        last = pe.transpose(dst[:, i * T + t * P:i * T + (t + 1) * P],
                                            src[:, t, (f0 + i) * P:(f0 + i + 1) * P], ident)
                last.then_inc(m_full, 1)

            def turn_rot(n=4):
                pe.wait_ge(rot_ready, s_rot(1))
                s_rot.step()
                for i in range(0, n, 2):
                    turn_two(rot, i)

            def logits(r, g):
                if l.k >= 1:
                    pe.wait_ge(l_free, l())
                if r == 0:
                    pe.wait_ge(m_free, m())
                for t in range(TT):
                    last = pe.matmul(L[:, t * P:t * P + P * (t + 1)], qT[:, r, t * P:(t + 1) * P],
                                     kT[:, bass.ds(g, 1), 0:P * (t + 1)].rearrange("p a t -> p (a t)"),
                                     start=True, stop=True)
                last.then_inc(l_full, 1)
                l.step()

            def turn_probs(r):
                pe.wait_ge(probs_ready, s_probs(1))
                s_probs.step()
                dst = turned_bank()
                for i in range(3):
                    last = pe.transpose(dst[:, i * P:(i + 1) * P], probs[:, r % 2, i * P:(i + 1) * P], ident)
                last.then_inc(m_full, 1)

            def mix(r, g, later):
                pe.wait_ge(m_free, m(-later))
                if o.k >= 1:
                    pe.wait_ge(o_free, o())
                at0 = (r % 2) * T
                val = [v_nat[:, s, bass.ds(g * HD, HD)] for s in range(TT)]
                pe.matmul(O[:, at0:at0 + P], probsT[:, r % 2, 0:P], val[0], start=True, stop=True)
                pe.matmul(O[:, at0 + P:at0 + T], probsT[:, r % 2, P:2 * P], val[0], start=True, stop=False)
                pe.matmul(O[:, at0 + P:at0 + T], probsT[:, r % 2, 2 * P:3 * P], val[1], start=False,
                          stop=True).then_inc(o_full, 1)
                o.step()

            def score(p):
                for h in score_heads(p):
                    dst = turned_bank()
                    side = slice(IDX_DIM * (h % 2), IDX_DIM * (h % 2) + IDX_DIM)
                    for t in range(TT):
                        last = pe.matmul(dst[:, t * P:t * P + P * (t + 1)], qiT[side, h // 2, t * P:(t + 1) * P],
                                         kiT[side, 0:P * (t + 1)], start=True, stop=True)
                    last.then_inc(m_full, 1)

            def turn(with_heads, g, scoring=False):
                for p in range(8):
                    if p % 4 == 0:
                        dst = bank_for_block()
                    chunk(0, p % 4, 4, dst)
                    if with_heads:
                        if p < 4:
                            logits(p, g)
                        if 1 <= p <= 4:
                            turn_probs(p - 1)
                        if 2 <= p <= 5:
                            mix(p - 2, g, 0 if p == 5 else 1)
                        if p == 6:
                            pe.wait_ge(o_free, o())
                            turn_two(o_gated, 0)
                            turn_two(o_gated, 2)
                    if scoring and p == 0:
                        turn_rot()
                    if scoring and 1 <= p <= 2:
                        score(p + 5)
                    if p == 7:
                        turn_rot()

            def tail_heads(g):
                for p in range(6):
                    if p < 4:
                        logits(p, g)
                    if 1 <= p <= 4:
                        turn_probs(p - 1)
                    if 2 <= p:
                        mix(p - 2, g, 0 if p == 5 else 1)
                    if p < 5:
                        yield
                pe.wait_ge(o_free, o())
                turn_two(o_gated, 0)
                turn_two(o_gated, 2)

            def turn_sum(b, read):
                pe.wait_ge(block_read, read)
                turn_two(x_new[:, b % 2], 0)
                turn_two(x_new[:, b % 2], 2)

            def project_out(order, late, steps):
                read, banks = nb(), {}
                for p, (b, kc) in enumerate(order):
                    if p == late:
                        for _ in steps:
                            pass
                        pe.wait_ge(m_free, m())
                    if b not in banks:
                        banks[b] = bank_for_block()
                    chunk(1, kc, 4, banks[b])
                    next(steps, None)
                    if p in TURN_AT:
                        turn_sum(TURN_AT.index(p), read + TURN_AT.index(p) + 1)

            def last_sum():
                read = nb(-1)
                yield
                turn_sum(3, read)
                yield
                pe.wait_ge(m_free, m())
                yield

            pe.wait_ge(first_in, 32)
            pe.transpose(turned_bank()[:, 0:KT], gain_rows[0:KT, :], ident[0:KT, 0:KT]).then_inc(m_full, 1)
            for h in range(KT // 2):
                if h % (KT // 4) == 0:
                    pe.wait_ge(x_in[h // (KT // 4)], 16 * TT)
                turn_two(x, 2 * h)
            pe.wait_ge(gains_in, 16 * N_GAIN_LOADS)
            pe.transpose(turned_bank()[:, 0:N_GAINS], gain_rows[:], ident[0:N_GAINS, 0:N_GAINS]).then_inc(m_full, 1)
            pe.wait_ge(m_free, m(-1))

            def index_keys():
                yield
                pe.wait_ge(rot_ready, s_rot(2))
                s_rot.step(2)
                dst = turned_bank()
                for t in range(TT):
                    last = pe.transpose(dst[:, t * P:(t + 1) * P], ki2[:, t, :], ident)
                last.then_inc(m_full, 1)
                yield

            def index_queries():
                yield
                turn_rot()
                yield

            def index_steps():
                pe.wait_ge(m_free, m())
                for p in range(8):
                    if p == 1:
                        turn_rot()
                    if p + 1 in SCORES_AT:
                        score(SCORES_AT.index(p + 1))
                    if p == 7:
                        score(5)
                    yield

            gemm(0, width=80)
            gemm(0, steps=index_keys())
            gemm(0, steps=index_queries())
            for layer in range(2):
                steps = last_sum() if layer else index_steps()
                gemm(0, steps=steps)
                gemm(0, steps=steps)
                if layer:
                    turn_rot()
                turn(False, 0, scoring=(layer == 0))
                for j in loop(pe, 1, GROUPS, {c: 8, nb: 2, m: 8, l: 4, o: 4, s_rot: 1, s_probs: 4}):
                    turn(True, j - 1)
                project_out(ORDER_12, 6, tail_heads(GROUPS - 1))

            s_op = Count()

            def operand():
                pe.wait_ge(for_pe, s_op(1))
                s_op.step()

            def turn_all(src, n):
                for h in range(n // 2):
                    turn_two(src, 2 * h)

            def memory_steps():
                yield from last_sum()
                pe.wait_ge(mem_in, 16 * TT)
                for h in range(KT // 2):
                    turn_two(mem_nat, 2 * h)
                    if h % 2:
                        yield

            steps = memory_steps()
            gemm(0, steps=steps)
            gemm(0, steps=steps)

            def turn_normed(*at):
                for p in range(4):
                    if p in at:
                        operand()
                        turn_all((pre_q, pre)[turned_normed.k % 2], 4)
                        turned_normed.step()
                    yield

            turned_normed = Count()
            pe.wait_ge(m_free, m())
            for at in ((0, 3), (2,), (2,), ()):
                gemm(1, steps=turn_normed(*at))

            def mem_steps(mv_read):
                pe.wait_ge(m_free, m())
                pe.wait_ge(block_read, mv_read)
                for h in range(MEM_HEADS):
                    pe.wait_ge(l_free, l())
                    for t in range(TT):
                        for e in range(2):
                            last = pe.matmul(L[:, t * T:(t + 1) * T], mqT[:, 2 * h + e, t * P:(t + 1) * P],
                                             mkT[:, 2 * h + e, :], start=(e == 0), stop=(e == 1))
                    last.then_inc(l_full, 1)
                    l.step()
                    yield
                    yield
                    pe.wait_ge(l_free, l())
                    dst = turned_bank()
                    for s in range(2):
                        for t in range(TT):
                            last = pe.transpose(dst[:, s * T + t * P:s * T + (t + 1) * P],
                                                m_probs[:, h % 2, t, s * P:(s + 1) * P], ident)
                    last.then_inc(m_full, 1)
                    yield
                    pe.wait_ge(m_free, m())
                    dst = turned_bank()
                    for e in range(2):
                        for s in range(2):
                            last = pe.matmul(dst[:, e * T:(e + 1) * T],
                                             mv[:, s, h * MEM_DH + e * P:h * MEM_DH + (e + 1) * P],
                                             m_probsT[:, h % 2, s, :], start=(s == 0), stop=(s == 1))
                    last.then_inc(m_full, 1)
                    yield

            def branch_beside(ready, steps, k0=0, to_end=True):
                pe.wait_ge(m_free, ready)
                for b in range(D // NB):
                    gemm(0, steps=steps)
                    gemm(1, MIX_KC, k0=k0, steps=steps)
                if to_end:
                    for _ in steps:
                        pass

            def gla_steps():
                dst = turned_bank()
                for t in range(TT):
                    last = pe.transpose(dst[0:16, t * P:(t + 1) * P], ga[:, t, :], ident)
                last.then_inc(m_full, 1)
                yield
                pe.wait_ge(m_free, m())
                pe.wait_ge(small_in, 64)
                for t in range(TT):
                    pe.wait_ge(l_free, l())
                    pe.matmul(L[:], gaT[:, t * P:(t + 1) * P], w_a2[:], start=True, stop=True).then_inc(l_full, 1)
                    l.step()
                    yield
                    yield
                    operand()
                    dst = turned_bank()
                    for h in range(GLA_HEADS):
                        last = pe.matmul(dst[:, 2 * h:2 * h + 2], log_a[:, h * P:(h + 1) * P], ends[:], start=True, stop=True)
                    last.then_inc(m_full, 1)
                    pe.wait_ge(l_free, l())
                    pe.matmul(L[:], cum64, log_a[:], start=True, stop=True).then_inc(l_full, 1)
                    l.step()
                    pe.wait_ge(o_free, o())
                    pe.matmul(O[:], after64, log_a[:], start=True, stop=True).then_inc(o_full, 1)
                    o.step()
                    yield
                    yield
                    operand()
                    for nat in (gq, gk):
                        dst = turned_bank()
                        for h in range(GLA_HEADS):
                            last = pe.transpose(dst[:, h * P:(h + 1) * P], nat[:, t, h * P:(h + 1) * P], ident)
                        last.then_inc(m_full, 1)
                    yield
                    pe.wait_ge(m_free, m())
                    dst = turned_bank()
                    for h in range(GLA_HEADS):
                        last = pe.matmul(dst[:, h * P:(h + 1) * P], keT[:, h * P:(h + 1) * P], qeT[:, h * P:(h + 1) * P],
                                         start=True, stop=True)
                    last.then_inc(m_full, 1)
                    yield
                    operand()
                    pe.wait_ge(l_free, l())
                    pe.wait_ge(o_free, o())
                    for half in range(2):
                        n = 2 * t + half
                        rows = slice(half * GLA_CHUNK, (half + 1) * GLA_CHUNK)
                        if n:
                            pe.wait_ge(m_free, m())
                        for h in range(GLA_HEADS):
                            dst = (L, O)[h // 2][rows, (h % 2) * GLA_DV:(h % 2 + 1) * GLA_DV]
                            last = pe.matmul(dst, sT[rows, h * P + half * GLA_CHUNK:h * P + (half + 1) * GLA_CHUNK],
                                             gv[rows, t, h * GLA_DV:(h + 1) * GLA_DV], start=True, stop=(n == 0))
                            if n:
                                last = pe.matmul(dst, qeT[:, h * P + half * GLA_CHUNK:h * P + (half + 1) * GLA_CHUNK],
                                                 state[:, h, :], start=False, stop=True)
                            if half and h % 2:
                                last.then_inc((l_full, o_full)[h // 2], 1)
                        if n < 3:
                            for pair in range(2):
                                dst = turned_bank()
                                for i in range(2):
                                    h = 2 * pair + i
                                    last = pe.matmul(dst[:, i * GLA_DV:(i + 1) * GLA_DV], kd[rows, h * P:(h + 1) * P],
                                                     gv[rows, t, h * GLA_DV:(h + 1) * GLA_DV], start=True, stop=True)
                                last.then_inc(m_full, 1)
                        if half == 0:
                            yield
                    l.step()
                    o.step()
                    yield
                    yield
                    yield
                    yield
                    s_op.step()

            def gr_steps():
                pe.wait_ge(for_pe, s_op())
                for h in range(4):
                    turn_two(gr, 2 * h)
                    yield

            def sb_steps():
                def turn_head(h):
                    dst = turned_bank()
                    for n, nat in enumerate((sq_nat, sk_nat)):
                        for t in range(TT):
                            last = pe.transpose(dst[:, n * T + t * P:n * T + (t + 1) * P], nat[:, h, t, :], ident)
                    last.then_inc(m_full, 1)

                def scores(i, later):
                    pe.wait_ge(m_free, m(-later))
                    pe.wait_ge(l_free, l())
                    pe.matmul(L[:, 0:T], qkT[:, i, 1, 0:P], qkT[:, i, 0, :], start=True, stop=True)
                    pe.matmul(L[:, T:W0], qkT[:, i, 1, P:T], qkT[:, i, 0, P:T], start=True, stop=True).then_inc(l_full, 1)
                    l.step()

                def sums(i):
                    operand()
                    pe.wait_ge(o_free, o())
                    pe.matmul(O[:, 0:W0], after, neg_l[:, i, :], start=True, stop=False)
                    pe.matmul(O[:, P:T], ones, neg_l[:, i, T:W0], start=False, stop=True).then_inc(o_full, 1)
                    o.step()

                for pair in range(SB_HEADS // 2):
                    turn_head(2 * pair)
                    yield
                    scores(0, 0)
                    turn_head(2 * pair + 1)
                    yield
                    yield
                    scores(1, 0)
                    sums(0)
                    yield
                    yield
                    sums(1)
                    yield
                    yield
                    operand()
                    operand()
                    dst = turned_bank()
                    for i in range(2):
                        h = 2 * pair + i
                        pe.matmul(dst[:, i * T:(i + 1) * T], sv_nat[:, 0, h * P:(h + 1) * P], stick[:, i, 0:T],
                                  start=True, stop=False)
                        last = pe.matmul(dst[:, i * T + P:(i + 1) * T], sv_nat[:, 1, h * P:(h + 1) * P],
                                         stick[:, i, T:W0], start=False, stop=True)
                    last.then_inc(m_full, 1)
                    yield

            steps = mem_steps(nb())
            gemm(0, width=16, steps=steps)
            for b in range(6):
                gemm(0, steps=steps)
            for _ in steps:
                pass
            branch_beside(m(), gla_steps())
            steps = gr_steps()
            gemm(0, steps=steps)
            for _ in steps:
                pass
            ready = m()
            gemm(0)

            def late_start():
                yield
                yield
                operand()
                yield from sb_steps()

            steps = late_start()
            for b in range(4):
                gemm(0, steps=steps)
            branch_beside(ready, steps)

            def merged_steps():
                for b, gap in enumerate(MERGED_GAPS):
                    for _ in range(gap):
                        yield
                    operand()
                    turn_two(x, 4 * b)
                    turn_two(x, 4 * b + 2)

            steps = merged_steps()
            branch_beside(m(), steps, k0=8, to_end=False)
            project_out(ORDER_8, 4, steps)
            for b0, n in FF_PARTS:
                def turn_mid(back):
                    pe.wait_ge(block_read, nb(back))
                    turn_all(f_mid, 4)

                def ffn_turn(prev, steps=iter(())):
                    for p in range(8):
                        if p % 4 == 0:
                            dst = bank_for_block()
                        chunk(0, p % 4, 4, dst)
                        next(steps, None)
                        if p == 2 and prev:
                            turn_mid(-1)

                def last_mid():
                    turn_mid(-1)
                    yield
                    pe.wait_ge(m_free, m())
                    yield

                ffn_turn(False, last_sum() if b0 == 0 else iter(()))
                for j in loop(pe, 1, n, {c: 8, nb: 2, m: 2}):
                    ffn_turn(True)
                steps = last_mid()
                for b in range(4):
                    gemm(1, n, steps=steps)


_INS = {
    "x": "x", "a_norm": "a_norm", "a_w_in": "a_w_in", "a_q_norm": "a_q_norm", "a_k_norm": "a_k_norm", "a_w_out": "a_w_out",
    "b_norm": "b_norm", "b_w_in": "b_w_in", "b_q_norm": "b_q_norm", "b_k_norm": "b_k_norm", "b_w_out": "b_w_out",
    "mem": "mem_2", "attn_norm_2": "attn_norm_2", "w_in": "w_in_2", "w_a2": "gla_w_a2_2", "b_a": "gla_b_a_2",
    "gla_norm": "gla_out_norm_2", "w_gla": "w_br_gla_2", "sb_q_norm": "sb_q_norm_2", "sb_k_norm": "sb_k_norm_2",
    "w_sb": "w_br_sb_2", "mem_norm_2": "mem_norm_2", "w_kv": "w_mem_kv_2", "mem_q_norm": "mem_q_norm_2",
    "mem_k_norm": "mem_k_norm_2", "w_mem": "w_br_mem_2", "w_o": "w_o_2", "ffn_norm_2": "ffn_norm_2",
    "w_gate_up": "w_gate_up_2", "w_down": "w_down_2",
}


def kernel(**inputs):
    import concourse.bacc as bacc
    from concourse.bass_utils import run_bass_kernel_spmd

    nc = bacc.Bacc("TRN2", target_bir_lowering=False, num_devices=1)
    arrays, io = {}, {}
    named = {name: np.ascontiguousarray(inputs[key]) for name, key in _INS.items()}
    named.update(constants())
    for name, a in named.items():
        arrays[f"in_{name}"] = a
        io[name] = nc.dram_tensor(f"in_{name}", a.shape, mybir.dt.from_np(a.dtype), kind="ExternalInput").ap()
    out = nc.dram_tensor("out_x", (1, T, D), F32, kind="ExternalOutput").ap()
    program(nc, io, out)
    r = run_bass_kernel_spmd(nc, [arrays], core_ids=[0])
    return r.results[0]["out_x"]
```
